# Optimizing a Trainium2 kernel written in Bass

```python
import math
import jax
import jax.numpy as jnp
from jax import lax
import numpy as np

D_MODEL = 1024
BATCH = 1
SEQ = 512
DEPTH = 2

HEAD_DIM = 64
DIFF_HEADS = 4
DIFF_V_DIM = 2 * HEAD_DIM
NSA_HEADS = 8
NSA_KV_GROUPS = 2
CMP_LEN = 32
CMP_STRIDE = 16
CMP_HIDDEN = 256
SLC_BLOCK = 64
SLC_TOPK = 16
NSA_WINDOW = 512
FORCED_SCORE = 1e4
SWA_HEADS = 8
SWA_KV_HEADS = 2
SWA_WINDOW = 128
N_BRANCHES = 3
BRANCH_WIDTH = SWA_HEADS * HEAD_DIM
D_FF = ((8 * D_MODEL // 3 + 255) // 256) * 256
PLE_DIM = 256
QUERY_BLOCK = 128
SLC_QUERY_CHUNK = 32
LN_EPS = 1e-5
SUBLN_EPS = 1e-5
ALPHA = (2 * DEPTH) ** 0.25
BETA = (8 * DEPTH) ** -0.25
NEG_INF = -1e30

IN_SPLITS = (
    DIFF_HEADS * 2 * HEAD_DIM,
    DIFF_HEADS * 2 * HEAD_DIM,
    DIFF_HEADS * DIFF_V_DIM,
    NSA_HEADS * HEAD_DIM,
    2 * NSA_KV_GROUPS * HEAD_DIM,
    2 * NSA_KV_GROUPS * HEAD_DIM,
    2 * NSA_KV_GROUPS * HEAD_DIM,
    3 * NSA_HEADS,
    SWA_HEADS * HEAD_DIM,
    SWA_KV_HEADS * HEAD_DIM,
    SWA_KV_HEADS * HEAD_DIM,
    N_BRANCHES * D_MODEL,
)
D_IN = sum(IN_SPLITS)

kernel_name = 'hybrid_diff_nsa_swa_macaron_deepnorm'

def _split_offsets():
    offs, acc = [], 0
    for n in IN_SPLITS[:-1]:
        acc += n
        offs.append(acc)
    return offs

def layer_norm(x, g, b):
    xf = x.astype(jnp.float32)
    mu = jnp.mean(xf, axis=-1, keepdims=True)
    var = jnp.mean(jnp.square(xf - mu), axis=-1, keepdims=True)
    return ((xf - mu) * lax.rsqrt(var + LN_EPS) * g + b).astype(x.dtype)

def swiglu(x, w_in, w_out):
    gate, up = jnp.split(x @ w_in, 2, axis=-1)
    return (jax.nn.silu(gate) * up) @ w_out

def alibi_slopes(n_heads):
    return jnp.exp2(-8.0 * jnp.arange(1, n_heads + 1, dtype=jnp.float32) / n_heads)

def diff_attention(q, k, v, lam, subln_g, lambda_init):
    B, H, S, _, d = q.shape
    scale = d ** -0.5
    lam = lam.astype(jnp.float32)
    lam_full = jnp.exp(jnp.dot(lam[0], lam[1])) - jnp.exp(jnp.dot(lam[2], lam[3])) + lambda_init
    slopes = alibi_slopes(H)[None, :, None, None, None]
    kpos = jnp.arange(S)

    def block(i):
        start = i * QUERY_BLOCK
        q_blk = lax.dynamic_slice_in_dim(q, start, QUERY_BLOCK, axis=2)
        dist = (start + jnp.arange(QUERY_BLOCK))[:, None] - kpos[None, :]
        s = jnp.einsum('bhqmd,bhkmd->bhmqk', q_blk, k, preferred_element_type=jnp.float32) * scale
        s = jnp.where(dist >= 0, s - slopes * dist, NEG_INF)
        a = jax.nn.softmax(s, axis=-1)
        w = a[:, :, 0] - lam_full * a[:, :, 1]
        return jnp.einsum('bhqk,bhkv->bhqv', w.astype(v.dtype), v)

    o = lax.map(block, jnp.arange(S // QUERY_BLOCK))
    o = jnp.moveaxis(o, 0, 2).reshape(B, H, S, -1).astype(jnp.float32)
    o = o * lax.rsqrt(jnp.mean(o * o, axis=-1, keepdims=True) + SUBLN_EPS) * subln_g
    return (o * (1.0 - lambda_init)).astype(v.dtype)

def banded_attention(q, k, v, slopes, window, sinks=None):
    B, G, R, S, d = q.shape
    scale = d ** -0.5
    span = QUERY_BLOCK + window
    kp = jnp.pad(k, ((0, 0), (0, 0), (window, 0), (0, 0)))
    vp = jnp.pad(v, ((0, 0), (0, 0), (window, 0), (0, 0)))
    sl = slopes.reshape(G, R)[None, :, :, None, None]

    def block(i):
        start = i * QUERY_BLOCK
        q_blk = lax.dynamic_slice_in_dim(q, start, QUERY_BLOCK, axis=3)
        k_blk = lax.dynamic_slice_in_dim(kp, start, span, axis=2)
        v_blk = lax.dynamic_slice_in_dim(vp, start, span, axis=2)
        qpos = start + jnp.arange(QUERY_BLOCK)
        kpos = start - window + jnp.arange(span)
        dist = qpos[:, None] - kpos[None, :]
        valid = (dist >= 0) & (dist < window) & (kpos[None, :] >= 0)
        s = jnp.einsum('bgrqd,bgkd->bgrqk', q_blk, k_blk, preferred_element_type=jnp.float32) * scale
        s = jnp.where(valid, s - sl * dist, NEG_INF)
        if sinks is None:
            a = jax.nn.softmax(s, axis=-1)
        else:
            sink = jnp.broadcast_to(sinks.astype(jnp.float32).reshape(G, R)[None, :, :, None, None],
                                    s.shape[:-1] + (1,))
            a = jax.nn.softmax(jnp.concatenate([s, sink], axis=-1), axis=-1)[..., :-1]
        return jnp.einsum('bgrqk,bgkd->bgrqd', a.astype(v_blk.dtype), v_blk)

    o = lax.map(block, jnp.arange(S // QUERY_BLOCK))
    return jnp.moveaxis(o, 0, 4).reshape(B, G, R, S, d)

def nsa_attention(q, kv_cmp, kv_slc, kv_win, gates, cmp_pos, cmp_w1, cmp_w2):
    B, G, R, S, d = q.shape
    scale = d ** -0.5
    slopes = alibi_slopes(G * R)
    sl = slopes.reshape(G, R)[None, :, :, None, None]
    tpos = jnp.arange(S)

    n_cmp = (S - CMP_LEN) // CMP_STRIDE + 1
    c_start = jnp.arange(n_cmp) * CMP_STRIDE
    idx = c_start[:, None] + jnp.arange(CMP_LEN)[None, :]
    blocks = kv_cmp[:, :, :, idx] + cmp_pos[:, None, None, None]
    hid = jax.nn.gelu(jnp.einsum('nbgcf,nfh->nbgch',
                                 blocks.reshape(2, B, G, n_cmp, CMP_LEN * d), cmp_w1))
    k_c, v_c = jnp.einsum('nbgch,nhd->nbgcd', hid, cmp_w2)
    dist_c = tpos[:, None] - (c_start + CMP_LEN - 1)[None, :]
    valid_c = dist_c >= 0
    s_c = jnp.einsum('bgrtd,bgcd->bgrtc', q, k_c, preferred_element_type=jnp.float32) * scale
    s_c = jnp.where(valid_c, s_c - sl * dist_c, NEG_INF)
    p_c = jax.nn.softmax(s_c, axis=-1) * jnp.any(valid_c, axis=-1)[:, None]
    o_cmp = jnp.einsum('bgrtc,bgcd->bgrtd', p_c.astype(v_c.dtype), v_c)

    n_blk = S // SLC_BLOCK
    n_sel = min(SLC_TOPK, n_blk)
    j_start = jnp.arange(n_blk) * SLC_BLOCK
    overlap = (jnp.minimum(c_start[:, None] + CMP_LEN, j_start[None, :] + SLC_BLOCK)
               - jnp.maximum(c_start[:, None], j_start[None, :]))
    cmp_to_slc = jnp.maximum(overlap, 0).astype(jnp.float32) / CMP_LEN
    score = jnp.einsum('bgrtc,cj->bgtj', p_c, cmp_to_slc)
    t_blk = (tpos // SLC_BLOCK)[:, None]
    jj = jnp.arange(n_blk)[None, :]
    score = jnp.where((jj == 0) | (jj == t_blk) | (jj == t_blk - 1), FORCED_SCORE, score)
    score = jnp.where(jj > t_blk, -1.0, score)
    _, sel = lax.top_k(score, n_sel)

    k_s, v_s = kv_slc
    k_blk = k_s.reshape(B, G, n_blk, SLC_BLOCK, d)
    v_blk = v_s.reshape(B, G, n_blk, SLC_BLOCK, d)
    bi = jnp.arange(B)[:, None, None, None]
    gi = jnp.arange(G)[None, :, None, None]
    C = SLC_QUERY_CHUNK
    n_keys = n_sel * SLC_BLOCK

    def chunk(i):
        start = i * C
        q_c = lax.dynamic_slice_in_dim(q, start, C, axis=3)
        sel_c = lax.dynamic_slice_in_dim(sel, start, C, axis=2)
        kg = k_blk[bi, gi, sel_c].reshape(B, G, C, n_keys, d)
        vg = v_blk[bi, gi, sel_c].reshape(B, G, C, n_keys, d)
        kpos = (sel_c[..., None] * SLC_BLOCK + jnp.arange(SLC_BLOCK)).reshape(B, G, C, n_keys)
        dist = ((start + jnp.arange(C))[None, None, :, None] - kpos)[:, :, None]
        s = jnp.einsum('bgrcd,bgckd->bgrck', q_c, kg, preferred_element_type=jnp.float32) * scale
        s = jnp.where(dist >= 0, s - sl * dist, NEG_INF)
        a = jax.nn.softmax(s, axis=-1)
        return jnp.einsum('bgrck,bgckd->bgrcd', a.astype(vg.dtype), vg)

    o_slc = lax.map(chunk, jnp.arange(S // C))
    o_slc = jnp.moveaxis(o_slc, 0, 4).reshape(B, G, R, S, d)

    k_w, v_w = kv_win
    o_win = banded_attention(q, k_w, v_w, slopes, NSA_WINDOW)

    return gates[0] * o_cmp + gates[1] * o_slc + gates[2] * o_win

def _kv_heads(t, groups):
    B, S, _ = t.shape
    return t.reshape(B, S, 2, groups, HEAD_DIM).transpose(2, 0, 3, 1, 4)

def token_mixing(x, w_in, diff_lam, diff_subln_g, cmp_pos, cmp_w1, cmp_w2, sinks,
                 w_branch, w_out, lambda_init):
    B, S, _ = x.shape
    d = HEAD_DIM
    (a_q, a_k, a_v, b_q, b_kvc, b_kvs, b_kvw, b_g,
     c_q, c_k, c_v, m_g) = jnp.split(x @ w_in, _split_offsets(), axis=-1)

    qa = a_q.reshape(B, S, DIFF_HEADS, 2, d).transpose(0, 2, 1, 3, 4)
    ka = a_k.reshape(B, S, DIFF_HEADS, 2, d).transpose(0, 2, 1, 3, 4)
    va = a_v.reshape(B, S, DIFF_HEADS, DIFF_V_DIM).transpose(0, 2, 1, 3)
    o_a = diff_attention(qa, ka, va, diff_lam, diff_subln_g, lambda_init)
    o_a = o_a.transpose(0, 2, 1, 3).reshape(B, S, BRANCH_WIDTH)

    G, R = NSA_KV_GROUPS, NSA_HEADS // NSA_KV_GROUPS
    qb = b_q.reshape(B, S, G, R, d).transpose(0, 2, 3, 1, 4)
    gb = jax.nn.sigmoid(b_g.reshape(B, S, 3, G, R)).transpose(2, 0, 3, 4, 1)[..., None]
    o_b = nsa_attention(qb, _kv_heads(b_kvc, G), _kv_heads(b_kvs, G), _kv_heads(b_kvw, G),
                        gb, cmp_pos, cmp_w1, cmp_w2)
    o_b = o_b.transpose(0, 3, 1, 2, 4).reshape(B, S, BRANCH_WIDTH)

    Gc, Rc = SWA_KV_HEADS, SWA_HEADS // SWA_KV_HEADS
    qc = c_q.reshape(B, S, Gc, Rc, d).transpose(0, 2, 3, 1, 4)
    kc = c_k.reshape(B, S, Gc, d).transpose(0, 2, 1, 3)
    vc = c_v.reshape(B, S, Gc, d).transpose(0, 2, 1, 3)
    o_c = banded_attention(qc, kc, vc, alibi_slopes(SWA_HEADS), SWA_WINDOW, sinks)
    o_c = o_c.transpose(0, 3, 1, 2, 4).reshape(B, S, BRANCH_WIDTH)

    y = jnp.einsum('bsnc,ncd->bsnd', jnp.stack([o_a, o_b, o_c], axis=2), w_branch)
    g = jax.nn.sigmoid(m_g.reshape(B, S, N_BRANCHES, D_MODEL))
    return jnp.einsum('bsnd,bsnd->bsd', g, y) @ w_out

def setup_inputs(seed: int = 0) -> dict:
    key = jax.random.key(seed)
    ks = jax.random.split(key, 17)
    f32 = jnp.float32

    def nrm(k, shape, scale):
        return jax.random.normal(k, shape, f32) * scale

    return {
        'x': nrm(ks[0], (BATCH, SEQ, D_MODEL), 1.0),
        'p': nrm(ks[1], (DEPTH, BATCH, SEQ, PLE_DIM), 1.0),
        'ffn_w_in': nrm(ks[2], (DEPTH, 2, D_MODEL, 2 * D_FF), D_MODEL ** -0.5),
        'ffn_w_out': nrm(ks[3], (DEPTH, 2, D_FF, D_MODEL), BETA * D_FF ** -0.5),
        'ln_g': 1.0 + nrm(ks[4], (DEPTH, 3, D_MODEL), 0.05),
        'ln_b': nrm(ks[5], (DEPTH, 3, D_MODEL), 0.02),
        'w_in': nrm(ks[6], (DEPTH, D_MODEL, D_IN), D_MODEL ** -0.5),
        'diff_lam': nrm(ks[7], (DEPTH, 4, HEAD_DIM), 0.1),
        'diff_subln_g': 1.0 + nrm(ks[8], (DEPTH, DIFF_V_DIM), 0.05),
        'nsa_cmp_pos': nrm(ks[9], (DEPTH, 2, CMP_LEN, HEAD_DIM), 0.1),
        'nsa_cmp_w1': nrm(ks[10], (DEPTH, 2, CMP_LEN * HEAD_DIM, CMP_HIDDEN), (CMP_LEN * HEAD_DIM) ** -0.5),
        'nsa_cmp_w2': nrm(ks[11], (DEPTH, 2, CMP_HIDDEN, HEAD_DIM), CMP_HIDDEN ** -0.5),
        'swa_sinks': nrm(ks[12], (DEPTH, SWA_HEADS), 0.5),
        'w_branch': nrm(ks[13], (DEPTH, N_BRANCHES, BRANCH_WIDTH, D_MODEL), BETA * BRANCH_WIDTH ** -0.5),
        'w_out': nrm(ks[14], (DEPTH, D_MODEL, D_MODEL), BETA * D_MODEL ** -0.5),
        'ple_w_in': nrm(ks[15], (DEPTH, PLE_DIM, D_MODEL), BETA * PLE_DIM ** -0.5),
        'ple_w_gate': nrm(ks[16], (DEPTH, D_MODEL, D_MODEL), D_MODEL ** -0.5),
    }

def reference(x, p, ffn_w_in, ffn_w_out, ln_g, ln_b, w_in, diff_lam, diff_subln_g,
              nsa_cmp_pos, nsa_cmp_w1, nsa_cmp_w2, swa_sinks, w_branch, w_out,
              ple_w_in, ple_w_gate):
    for i in range(DEPTH):
        lambda_init = 0.8 - 0.6 * math.exp(-0.3 * i)
        x = layer_norm(ALPHA * x + 0.5 * swiglu(x, ffn_w_in[i, 0], ffn_w_out[i, 0]),
                       ln_g[i, 0], ln_b[i, 0])
        mix = token_mixing(x, w_in[i], diff_lam[i], diff_subln_g[i], nsa_cmp_pos[i],
                           nsa_cmp_w1[i], nsa_cmp_w2[i], swa_sinks[i], w_branch[i],
                           w_out[i], lambda_init)
        x = layer_norm(ALPHA * x + mix, ln_g[i, 1], ln_b[i, 1])
        h = ALPHA * x + 0.5 * swiglu(x, ffn_w_in[i, 1], ffn_w_out[i, 1])
        h = h + jax.nn.sigmoid(h @ ple_w_gate[i]) * (p[i] @ ple_w_in[i])
        x = layer_norm(h, ln_g[i, 2], ln_b[i, 2])
    return x


_drawn_inputs = setup_inputs


def setup_inputs(seed=0):
    import zlib

    import numpy as np

    out = dict(_drawn_inputs(seed))
    spreads = {}
    factors = {'diff_lam': 3.821, 'diff_subln_g': 8.0, 'nsa_cmp_pos': 8.0, 'swa_sinks': 8.0}
    for name, (base, spread) in spreads.items():
        noise = np.random.default_rng([zlib.crc32(name.encode()), seed]).standard_normal(out[name].shape)
        drawn = base * np.exp(spread * noise) if base else spread * noise
        out[name] = jnp.asarray(drawn.astype(out[name].dtype))
    for name, factor in factors.items():
        out[name] = (out[name] * factor).astype(out[name].dtype)
    return out
```

```python
import math
from contextlib import ExitStack

import numpy as np

import concourse.bass as bass
from concourse import mybir

F32 = mybir.dt.float32
F32R = mybir.dt.float32r
ALU = mybir.AluOpType
ACT = mybir.ActivationFunctionType
AX = mybir.AxisListType

P = 128
D = 1024
SEQ = 512
DEPTH = 2
HD = 64
D_FF = 2816
PLE = 256
KT = D // P
FT = D_FF // P
TT = SEQ // P
ALPHA = (2 * DEPTH) ** 0.25
EPS = 1e-5
SCALE = HD ** -0.5
BIG = 1e32
N_CMP = (SEQ - 32) // 16 + 1
UNIT = KT * P

A_Q, A_K, A_V, B_Q, B_KVC, B_KVS, B_KVW, B_G, C_Q, C_K, C_V, M_G = (
    0, 512, 1024, 1536, 2048, 2304, 2560, 2816, 2840, 3352, 3480, 3608)

PAIRS_FFN_IN, PAIRS_FFN_OUT, PAIRS_FM, PAIRS_TM, PAIRS_MIX, PAIRS_WOUT, PAIRS_PLE, PAIRS_PGATE = (
    FT, FT // 2, 12, 4, 24, 4, 2, 4)
P_FFN1 = 0
P_OUT1 = P_FFN1 + PAIRS_FFN_IN
P_FM = P_OUT1 + PAIRS_FFN_OUT
P_TM = P_FM + PAIRS_FM
P_MIX = P_TM + PAIRS_TM
P_WOUT = P_MIX + PAIRS_MIX
P_FFN2 = P_WOUT + PAIRS_WOUT
P_OUT2 = P_FFN2 + PAIRS_FFN_IN
P_PLE = P_OUT2 + PAIRS_FFN_OUT
P_PGATE = P_PLE + PAIRS_PLE
PAIRS = P_PGATE + PAIRS_PGATE
assert PAIRS % 2 == 0
CREDIT = 2

FM_QB, FM_QC, FM_QA, FM_KA, FM_KS, FM_KW, FM_KC = 0, 4, 8, 12, 16, 17, 18
FM = 19
V_A, V_S, V_W, V_C, V_END = 0, 512, 640, 768, 896

LN_G, LN_B, LAM, SINK, SUBG, LINIT, POS = 0, 24, 48, 304, 312, 313, 316
N_PAR = POS + 64
C_D, C_SWA, C_CMP, C_ID, C_ONE, C_SLOPE, C_VALID = 0, 512, 768, 896, 1024, 1152, 1168
N_CST = C_VALID + 8

SLC, WIN, SWA, DIFF = range(4)
UNITS = [(kind, i, a) for kind in (SLC, WIN, SWA, DIFF) for i in range(TT) for a in range(2)]
N_U = len(UNITS)
PU = [n for n, (kind, i, a) in enumerate(UNITS) if kind != DIFF or a == 1]
N_P = len(PU)
PIDX = {n: p for p, n in enumerate(PU)}


N_MERGE, N_CS, N_SUB = 14, 7, 5
M_SLC, M_WIN, M_SWA, M_DIFF = 4, 7, 10, 12
N_FM = FM + 2
Y_LAYER = 7 + 4 + 7 + 7


def key_blocks(kind, i):
    return list(range(max(0, i - 1), i + 1)) if kind == SWA else list(range(i + 1))


def build(nc, xT, pT, cst_d, par_d, w1_d, w2_d, ffn_in, ffn_out, proj_fm, proj_tm, mix, wout, ple_in, ple_gate, out):
    ctx = ExitStack()
    with ctx:
        def sb(name, shape, dt=F32, stack=ctx):
            return stack.enter_context(nc.sbuf_tensor(name, shape, dt))

        def sem(name):
            return ctx.enter_context(nc.semaphore(name))

        xa = sb("xa", [P, KT, SEQ])
        x_hi = sb("x_hi", [P, KT, SEQ], F32R)
        x_lo = sb("x_lo", [P, KT, SEQ], F32R)
        raw = sb("raw", [P, 2, 2 * UNIT])
        w_hi = sb("w_hi", [P, 4, UNIT], F32R)
        w_lo = sb("w_lo", [P, 4, UNIT], F32R)
        cst = sb("cst", [P, N_CST])
        par = sb("par", [P, N_PAR])
        tmp = sb("tmp", [P, 4, SEQ])
        sq = tmp[:, 0:2, :]
        std = sb("std", [P, SEQ])
        rstd = sb("rstd", [P, SEQ])
        credit = sb("credit", [P, 16])
        eps_c = sb("eps_c", [P, 1])
        warm = sb("warm", [P, 1])
        par_a = sb("par_a", [P, 6 * KT])

        with ExitStack() as st:
            h_hi = sb("h_hi", [P, FT, SEQ], F32R, st)
            h_lo = sb("h_lo", [P, FT, SEQ], F32R, st)
        sil, hf = sq, tmp[:, 2:4, :]
        with ExitStack() as st:
            p_f = sb("p_f", [P, 2, SEQ], F32, st)
            p_hi = sb("p_hi", [P, 2, SEQ], F32R, st)
            p_lo = sb("p_lo", [P, 2, SEQ], F32R, st)
            pp = sb("pp", [P, KT, SEQ], F32, st)
            pg = sb("pg", [P, 2, SEQ], F32, st)
            pgp = sb("pgp", [P, 2, SEQ], F32, st)
        with ExitStack() as st:
            fm = sb("fm", [P, FM, SEQ], F32, st)
            vt = sb("vt", [P, TT, V_END], F32, st)
            gate = sb("gate", [P, 3, TT, 2, 4], F32, st)
            hid = sb("hid", [P, 4, 64], F32, st)
            hid_b = sb("hid_b", [P, 4], F32, st)
            w2 = sb("w2", [P, 4, HD], F32, st)
            kcmp = sb("kcmp", [P, 32], F32, st)
            vcmp = sb("vcmp", [P, 4, HD], F32, st)
            neglam = sb("neglam", [P, 4], F32, st)
            subg = sb("subg", [P, 1], F32, st)
            ms = sb("ms", [P, 4, TT], F32, st)
            msr = sb("msr", [P, 4, TT], F32, st)
            msr2 = sb("msr2", [P, 4, TT], F32, st)
            lam_t = sb("lam_t", [P, 2, HD], F32, st)
            nmx = sb("nmx", [P, N_U], F32, st)
            lsum = sb("lsum", [P, N_U], F32, st)
            rl = sb("rl", [P, N_U], F32, st)
            fac = sb("fac", [P, 4, 8], F32, st)
            cmx = sb("cmx", [P, 8], F32, st)
            csum = sb("csum", [P, 8], F32, st)
            crl = sb("crl", [P, 8], F32, st)
            cfac = sb("cfac", [P, 2, 8], F32, st)
            sk = sb("sk", [P, 2], F32, st)
            nsk = sb("nsk", [P, 2], F32, st)
            esk = sb("esk", [P, TT, 2], F32, st)
            lswa = sb("lswa", [P, 8], F32, st)
            dfac = sb("dfac", [P, TT], F32, st)
            with ExitStack() as s2:
                w1 = sb("w1", [P, 2, 16, 256], F32, s2)
            with ExitStack() as s2:
                pt = sb("pt", [P, 2, SEQ], F32, s2)
                qst = sb("qst", [P, 3, SEQ], F32, s2)
                kst = sb("kst", [P, SEQ], F32, s2)
                bias_f = sb("bias_f", [P, 2, SEQ], F32, s2)
                bias_s = sb("bias_s", [P, 2, 256], F32, s2)
                bias_c = sb("bias_c", [P, TT, 2, 32], F32, s2)
                cs = sb("cs", [P, TT, 2, 32], F32, s2)
                cs2 = sb("cs2", [P, TT, 2, 32], F32, s2)
                cp = sb("cp", [P, TT, 2, 32], F32, s2)
                cpt = sb("cpt", [P, 2, P], F32, s2)
                o_cmp = sb("o_cmp", [P, SEQ], F32, s2)
                o_slc = sb("o_slc", [P, SEQ], F32, s2)
                o_a = sb("o_a", [P, 4, SEQ], F32, s2)
        with ExitStack() as st:
            z_hi = sb("z_hi", [P, KT, SEQ], F32R, st)
            z_lo = sb("z_lo", [P, KT, SEQ], F32R, st)
            ob_hi = sb("ob_hi", [P, 12, SEQ], F32R, st)
            ob_lo = sb("ob_lo", [P, 12, SEQ], F32R, st)
            sg = sb("sg", [P, 3, SEQ], F32, st)
            gy = sb("gy", [P, SEQ], F32, st)
            zt = sb("zt", [P, 2, SEQ], F32, st)
        bias_d, otmp = std, rstd
        o_win, o_c = rstd, o_cmp
        gfm, gfm_slc = rstd[0:24, :], std[0:24, :]
        gat = tmp[:, :, :].rearrange("p a b -> p (a b)").rearrange("p (n j c) -> p n j c", n=2, j=16)
        nS, pE = sq, tmp[:, 2:4, :]

        pb = ctx.enter_context(nc.psum_tensor("pb", [P, 8, SEQ], F32))

        ident = cst[:, C_ID:C_ID + P]
        ones = cst[:, C_ONE:C_ONE + P]

        constants = sem("constants")
        par_loaded = sem("par_loaded")
        w1_loaded = sem("w1_loaded")
        p_loaded = sem("p_loaded")
        raw_loaded = [sem(f"raw_loaded_{i}") for i in range(2)]
        pair_split = sem("pair_split")
        pair_hi = sem("pair_hi")
        pair_done = sem("pair_done")
        eps_set = sem("eps_set")
        x_hi_done = sem("x_hi_done")
        x_ready = sem("x_ready")
        xa_done = sem("xa_done")
        gate_done = sem("gate_done")
        silu_done = sem("silu_done")
        gate_up_free = sem("gate_up_free")
        h_hi_done = sem("h_hi_done")
        h_ready = sem("h_ready")
        y_done = sem("y_done")
        resid_ready = sem("resid_ready")
        mean_done = sem("mean_done")
        centered = sem("centered")
        squared = sem("squared")
        var_step = sem("var_step")
        std_done = sem("std_done")
        rstd_done = sem("rstd_done")
        normed = sem("normed")
        affine = sem("affine")
        par_scaled = sem("par_scaled")
        proj_even = sem("proj_even")
        proj_free = sem("proj_free")
        gathered = sem("gathered")
        hid_done = sem("hid_done")
        hid_bias = sem("hid_bias")
        hid_ready = sem("hid_ready")
        cmp_kv_done = sem("cmp_kv_done")
        vcmp_zeroed = sem("vcmp_zeroed")
        cmp_kv = sem("cmp_kv")
        v_done = sem("v_done")
        v_ready = sem("v_ready")
        v_ready_b = sem("v_ready_b")
        neglam_ready = sem("neglam_ready")
        lam_step = sem("lam_step")
        lam_exp = sem("lam_exp")
        staged = sem("staged")
        bias_made = sem("bias_made")
        scores_done = sem("scores_done")
        negmax_done = sem("negmax_done")
        exp_done = sem("exp_done")
        diff_fac = sem("diff_fac")
        diff_combined = sem("diff_combined")
        pt_done = sem("pt_done")
        pt_copied = sem("pt_copied")
        pv_done = sem("pv_done")
        cmp_scores = sem("cmp_scores")
        cmp_step = sem("cmp_step")
        cmp_exp = sem("cmp_exp")
        cmp_turned = sem("cmp_turned")
        cmp_pt = sem("cmp_pt")
        cmp_pv = sem("cmp_pv")
        sink_exp = sem("sink_exp")
        merge_step = sem("merge_step")
        ot_done = sem("ot_done")
        ot_copied = sem("ot_copied")
        sub_step = sem("sub_step")
        sub_std = sem("sub_std")
        ob_hi_done = sem("ob_hi_done")
        ob_ready = sem("ob_ready")
        mix_gate = sem("mix_gate")
        sig_done = sem("sig_done")
        mix_free = sem("mix_free")
        mix_step = sem("mix_step")
        z_hi_done = sem("z_hi_done")
        z_ready = sem("z_ready")
        p_split = sem("p_split")
        pp_ready = sem("pp_ready")
        hs_hi = sem("hs_hi")
        hs_ready = sem("hs_ready")
        pgate_even = sem("pgate_even")
        pg_done = sem("pg_done")
        pg_mul = sem("pg_mul")
        resid3 = sem("resid3")
        final_done = sem("final_done")
        stored = sem("stored")
        passed_pe, passed_act, passed_dve, passed_pool = (sem(f"passed_{e}") for e in ("pe", "act", "dve", "pool"))

        block = ctx.enter_context(nc.Block())
        NCONST = 16 * 2

        def in_order(ap, br, i):
            if br == 0:
                return ap[:, i * P:(i + 1) * P]
            if br == 1:
                return ap.rearrange("p (c h) -> p h c", h=16)[:, 4 * i:4 * i + 4, :]
            return ap.rearrange("p (c h) -> p h c", h=4)[:, i, :]

        def pairs(L, p):
            return L * PAIRS + (p + 1 + CREDIT)

        segments = [
            (ffn_in, PAIRS_FFN_IN, lambda L: L * (2 * PAIRS_FFN_IN), 2 * UNIT),
            (ffn_out, PAIRS_FFN_OUT, lambda L: L * (2 * PAIRS_FFN_OUT), 2 * UNIT),
            (proj_fm, PAIRS_FM, lambda L: L * PAIRS_FM, 2 * UNIT),
            (proj_tm, PAIRS_TM, lambda L: L * PAIRS_TM, 2 * UNIT),
            (mix, PAIRS_MIX, lambda L: L * PAIRS_MIX, UNIT + UNIT // 2),
            (wout, PAIRS_WOUT, lambda L: L * PAIRS_WOUT, 2 * UNIT),
            (ffn_in, PAIRS_FFN_IN, lambda L: L * (2 * PAIRS_FFN_IN) + PAIRS_FFN_IN, 2 * UNIT),
            (ffn_out, PAIRS_FFN_OUT, lambda L: L * (2 * PAIRS_FFN_OUT) + PAIRS_FFN_OUT, 2 * UNIT),
            (ple_in, PAIRS_PLE, lambda L: L * PAIRS_PLE, UNIT),
            (ple_gate, PAIRS_PGATE, lambda L: L * PAIRS_PGATE, 2 * UNIT),
        ]

        @block.sync
        def _(sp):
            sp.dma_start(xa[:, :, :], xT).then_inc(constants, 16)
            sp.dma_start(cst[:, :], cst_d).then_inc(constants, 16)

            with sp.Fori(0, DEPTH) as L:
                p0 = 0
                for arr, n, first, width in segments:
                    def load(j, p):
                        sp.wait_ge(pair_split, L * PAIRS + j + (p + 1))
                        sp.dma_start(raw[:, p % 2, 0:width], arr[first(L) + j + (p - p0)]).then_inc(raw_loaded[p % 2], 16)

                    with sp.Fori(0, n // 2) as half:
                        j = half * 2
                        load(j, p0)
                        load(j, p0 + 1)
                    if n % 2:
                        load(0, p0 + n - 1)
                    p0 += n
            sp.wait_ge(final_done, KT)
            sp.dma_start(out, xa[:, :, :]).then_inc(stored, 16)
            sp.wait_ge(stored, 16)

        @block.gpsimd
        def _(pool):
            for slot in range(CREDIT):
                nc.gpsimd.memset(credit[:, 2 * slot:2 * slot + 1], 0.0).then_inc(pair_split, 1)
                nc.gpsimd.memset(credit[:, 2 * slot + 1:2 * slot + 2], 0.0).then_inc(pair_done, 1)
            pool.wait_ge(constants, NCONST)
            with pool.Fori(0, DEPTH) as L:
                p0 = 0
                for arr, n, first, width in segments:
                    def split(j, p):
                        s = 2 * (p % 2)
                        src = raw[:, p % 2, 0:width]
                        hi = w_hi[:, s:s + 2, :].rearrange("p a b -> p (a b)")[:, 0:width]
                        lo = w_lo[:, s:s + 2, :].rearrange("p a b -> p (a b)")[:, 0:width]
                        pool.wait_ge(pair_done, L * PAIRS + j + (p + 1))
                        pool.wait_ge(raw_loaded[p % 2], L * (8 * PAIRS) + j * 8 + 16 * (p // 2 + 1))
                        pool.sem_inc(passed_pool, 1)
                        nc.gpsimd.tensor_scalar(hi, src, 1.0, 1.0, ALU.mult, ALU.mult).then_inc(pair_hi, 1)
                        pool.wait_ge(pair_hi, L * PAIRS + j + (p + 1))
                        nc.gpsimd.tensor_tensor(lo, src, hi, ALU.subtract).then_inc(pair_split, 1)

                    with pool.Fori(0, n // 2) as half:
                        j = half * 2
                        split(j, p0)
                        split(j, p0 + 1)
                    if n % 2:
                        split(0, p0 + n - 1)
                    p0 += n

        @block.tensor
        def _(pe):

            def mm3(o, wh, wl, xh, xl, start, stop):
                nc.tensor.matmul(o, wh, xh, start=start, stop=False, skip_group_check=True)
                nc.tensor.matmul(o, wh, xl, start=False, stop=False, skip_group_check=True)
                return nc.tensor.matmul(o, wl, xh, start=False, stop=stop, skip_group_check=True)

            def blk(slot, b):
                return w_hi[:, slot, b * P:(b + 1) * P], w_lo[:, slot, b * P:(b + 1) * P]

            def unit_mm(bank, slot, hi, lo, nk=KT):
                for k in range(nk):
                    last = mm3(pb[:, bank, :], *blk(slot, k), hi[:, k, :], lo[:, k, :], k == 0, k == nk - 1)
                return last

            def as_x_comes(L, n_x, bank, slot, first_done):
                for k in range(KT):
                    pe.wait_ge(x_ready, L * (3 * KT) + (n_x * KT + k + 1))
                    for u in range(2):
                        last = mm3(pb[:, bank + u, :], *blk(slot + u, k), x_hi[:, k, :], x_lo[:, k, :], k == 0,
                                   k == KT - 1)
                        if k == KT - 1:
                            last.then_inc((first_done, pair_done)[u], 1)

            def split_wait(L, j, p):
                pe.wait_ge(pair_split, L * PAIRS + j + (p + 1 + CREDIT))

            def ffn(L, f, pin, pout, n_x):
                def tile(m, n):
                    b, s = 2 * (n % 2), 2 * ((pin + n) % 2)
                    split_wait(L, m, pin + n)
                    pe.wait_ge(gate_up_free, L * (2 * FT) + m + (f * FT + n + 1))
                    unit_mm(b, s, x_hi, x_lo).then_inc(gate_done, 1)
                    unit_mm(b + 1, s + 1, x_hi, x_lo).then_inc(pair_done, 1)

                split_wait(L, 0, pin)
                pe.wait_ge(gate_up_free, L * (2 * FT) + (f * FT + 1))
                as_x_comes(L, n_x, 0, 2 * (pin % 2), gate_done)
                tile(0, 1)
                with pe.Fori(0, FT // 2 - 1) as half:
                    tile(half * 2, 2)
                    tile(half * 2, 3)

                def out_pair(j, p, k0, first, last):
                    s = 2 * (p % 2)
                    split_wait(L, j, p)
                    pe.wait_ge(h_ready, L * (2 * FT) + j * 2 + (f * FT + 2 * (k0 + 1)))
                    if first:
                        order = [(u, m) for u in range(2) for m in (4, 5, 6, 7, 0, 1, 2, 3)]
                    elif last:
                        order = [(u, m) for m in range(KT) for u in range(2)]
                    else:
                        order = [(u, m) for u in range(2) for m in range(KT)]
                    for n, (u, m) in enumerate(order):
                        if first and n == 4:
                            pe.wait_ge(gate_up_free, L * (2 * FT) + (f * FT + FT + 2))
                        k = j * 2 + (2 * k0 + u)
                        mm = mm3(pb[:, m, :], *blk(s + u, m), h_hi[:, k, :], h_lo[:, k, :],
                                 first and u == 0, last and u == 1)
                        if last and u == 1 and m < KT - 1:
                            mm.then_inc(y_done, 1)
                    mm.then_inc(pair_done, 1)

                out_pair(0, pout, 0, True, False)
                with pe.Fori(0, 4) as half:
                    j = half * 2
                    out_pair(j, pout + 1, 1, False, False)
                    out_pair(j, pout + 2, 2, False, False)
                out_pair(0, pout + 9, 9, False, False)
                out_pair(0, pout + 10, 10, False, True)

            def norm(L, n, src, base, per_layer):
                for m in range(KT):
                    pe.wait_ge(src, L * per_layer + (base + m + 1))
                    mm = nc.tensor.matmul(pb[:, 0, :], ones, xa[:, m, :], start=m == 0, stop=m == KT - 1)
                mm.then_inc(mean_done, 1)
                for m in range(KT):
                    pe.wait_ge(squared, L * (3 * KT) + (n * KT + m + 1))
                    nc.tensor.matmul(pb[:, 1, :], ones, sq[:, m % 2, :], start=m == 0,
                                     stop=m == KT - 1).then_inc(var_step, 1)

            def projections(L):
                split_wait(L, 0, P_FM)
                as_x_comes(L, 1, 0, 2 * (P_FM % 2), proj_even)
                s = 2 * ((P_FM + 1) % 2)
                split_wait(L, 0, P_FM + 1)
                unit_mm(2, s, x_hi, x_lo).then_inc(proj_even, 1)
                unit_mm(3, s + 1, x_hi, x_lo).then_inc(pair_done, 1)
                pe.wait_ge(gathered, L * 9 + 9)
                pe.sem_inc(passed_pe, 1)
                with pe.Fori(0, 4) as half:
                    j = half * 2
                    for q in range(2):
                        p = P_FM + 2 + q
                        s = 2 * (p % 2)
                        split_wait(L, j, p)
                        pe.wait_ge(proj_free, L * N_FM + j * 2 + (2 * q + 2))
                        unit_mm(2 * q, s, x_hi, x_lo).then_inc(proj_even, 1)
                        unit_mm(2 * q + 1, s + 1, x_hi, x_lo).then_inc(pair_done, 1)
                p = P_FM + 10
                s = 2 * (p % 2)
                split_wait(L, 0, p)
                pe.wait_ge(proj_free, L * N_FM + 18)
                unit_mm(0, s, x_hi, x_lo).then_inc(proj_even, 1)
                unit_mm(1, s + 1, x_hi, x_lo).then_inc(pair_done, 1)
                p = P_FM + 11
                s = 2 * (p % 2)
                split_wait(L, 0, p)
                pe.wait_ge(proj_free, L * N_FM + 20)
                unit_mm(2, s, x_hi, x_lo).then_inc(proj_even, 1)
                for k in range(KT):
                    mm = mm3(pb[0:24, 3, :], w_hi[:, s + 1, k * P:k * P + 24], w_lo[:, s + 1, k * P:k * P + 24],
                             x_hi[:, k, :], x_lo[:, k, :], k == 0, k == KT - 1)
                mm.then_inc(pair_done, 1)

                pe.wait_ge(w1_loaded, L * 32 + 32)
                for n in range(2):
                    for hm in range(2):
                        for j in range(16):
                            mm = nc.tensor.matmul(pb[:, 4 + 2 * n + hm, 0:64], w1[:, n, j, hm * P:(hm + 1) * P],
                                                  gat[:, n, j, :], start=j == 0, stop=j == 15)
                        mm.then_inc(hid_done, 1)
                pe.wait_ge(hid_ready, L * 4 + 4)
                pe.wait_ge(proj_free, L * N_FM + (N_FM + 4))
                pe.sem_inc(passed_pe, 1)
                for br in range(3):
                    for i in range(TT):
                        mm = nc.tensor.transpose(pb[:, 2, (br * TT + i) * 24:(br * TT + i + 1) * 24],
                                                 in_order(gfm_slc, 0, i) if br == 1 else in_order(gfm, br, i),
                                                 ident[0:24, 0:24])
                for g in range(2):
                    for hm in range(2):
                        nc.tensor.matmul(pb[64 * g:64 * g + 64, 0, 0:N_CMP], w2[:, hm, :],
                                         hid[:, hm, g * N_CMP:(g + 1) * N_CMP], start=hm == 0, stop=hm == 1)
                for r in range(4):
                    for hm in range(2):
                        g = r % 2
                        mm = nc.tensor.matmul(pb[32 * r:32 * r + N_CMP, 1, 0:HD],
                                              hid[:, 2 + hm, g * N_CMP:(g + 1) * N_CMP], w2[:, 2 + hm, :],
                                              start=hm == 0, stop=hm == 1)
                mm.then_inc(cmp_kv_done, 1)
                pe.wait_ge(cmp_kv, L * 8 + 8)

                for pr in range(PAIRS_TM):
                    p = P_TM + pr
                    s = 2 * (p % 2)
                    split_wait(L, 0, p)
                    last = pr == PAIRS_TM - 1
                    ui = [(u, i) for i in range(TT) for u in range(2)] if last else \
                         [(u, i) for u in range(2) for i in range(TT)]
                    for u, i in ui:
                        k = 2 * pr + u
                        xh, xl = x_hi[:, k, i * P:(i + 1) * P], x_lo[:, k, i * P:(i + 1) * P]
                        for b, c0, c1 in ((2 * i, 0, 512), (2 * i + 1, 512, V_END)):
                            mm = mm3(pb[:, b, 0:c1 - c0], xh, xl, w_hi[:, s + u, c0:c1], w_lo[:, s + u, c0:c1],
                                     k == 0, k == KT - 1)
                        if last and u == 1 and i < TT - 1:
                            mm.then_inc(v_done, 1)
                    mm.then_inc(pair_done, 1)

            def feature_major(bank, o, br, i, start, stop):
                dst = in_order(pb[:, bank, :], br, i)
                rhs = ident.rearrange("p (a b) -> p a b", a=4) if br == 1 else ident
                return nc.tensor.matmul(dst, o[:, i * P:(i + 1) * P], rhs, start=start, stop=stop,
                                        skip_group_check=True)

            def attention(L):
                pe.wait_ge(v_ready, L * TT + TT)
                pe.wait_ge(v_ready_b, L * TT + TT)
                pe.wait_ge(neglam_ready, L * 3 + 3)
                pe.sem_inc(passed_pe, 1)
                with pe.Fori(0, 4) as t:
                    e_u = L * (4 * N_U) + t * N_U
                    e_p = L * (4 * N_P) + t * N_P
                    e_1 = L * 4 + t
                    pe.wait_ge(staged, L * 16 + t * 4 + 4)

                    def scores(n):
                        kind, i, a = UNITS[n]
                        h = slice(64 * a, 64 * a + 64)
                        q = qst[h, {SLC: 0, WIN: 0, SWA: 1, DIFF: 2}[kind], i * P:(i + 1) * P]
                        b = key_blocks(kind, i)
                        ks = slice(b[0] * P, (b[-1] + 1) * P)
                        k = {SLC: fm[h, FM_KS, ks], WIN: fm[h, FM_KW, ks], SWA: fm[h, FM_KC, ks],
                             DIFF: kst[h, ks]}[kind]
                        if n >= 2:
                            pe.wait_ge(negmax_done, e_u + (n - 1))
                        nc.tensor.matmul(pb[:, n % 2, 0:len(b) * P], q, k, start=True,
                                         stop=True).then_inc(scores_done, 1)

                    def turn(n):
                        if n not in PIDX:
                            return
                        p = PIDX[n]
                        kind, i, a = UNITS[n]
                        if kind == DIFF:
                            pe.wait_ge(diff_combined, L * 16 + t * 4 + (i + 1))
                        else:
                            pe.wait_ge(exp_done, e_u + (n + 1))
                        if p >= 2:
                            pe.wait_ge(pt_copied, e_p + (p - 1))
                        for j in range(len(key_blocks(kind, i))):
                            mm = nc.tensor.transpose(pb[:, 2 + p % 2, j * P:(j + 1) * P],
                                                     pE[:, n % 2, j * P:(j + 1) * P], ident)
                        mm.then_inc(pt_done, 1)

                    def pv(n):
                        if n not in PIDX:
                            return
                        p = PIDX[n]
                        kind, i, a = UNITS[n]
                        pe.wait_ge(pt_copied, e_p + (p + 1))
                        blocks = key_blocks(kind, i)
                        for j, b in enumerate(blocks):
                            if kind == DIFF:
                                o, v = pb[:, 6, i * P:(i + 1) * P], vt[:, b, bass.ts(t, P)]
                            else:
                                c = {SLC: V_S, WIN: V_W, SWA: V_C}[kind] + 64 * a
                                o = pb[:, {SLC: 4, WIN: 5, SWA: 7}[kind], (2 * i + a) * HD:(2 * i + a + 1) * HD]
                                v = vt[:, b, c:c + HD]
                            mm = nc.tensor.matmul(o, pt[:, p % 2, j * P:(j + 1) * P], v, start=j == 0,
                                                  stop=j == len(blocks) - 1)
                        mm.then_inc(pv_done, 1)

                    for i in range(TT):
                        for a in range(2):
                            h = slice(64 * a, 64 * a + 64)
                            mm = nc.tensor.matmul(pb[:, 6 + a, i * 32:(i + 1) * 32], qst[h, 0, i * P:(i + 1) * P],
                                                  kcmp[h, :], start=True, stop=True)
                    mm.then_inc(cmp_scores, 1)
                    for n in range(N_U + 3):
                        if n < N_U:
                            scores(n)
                        if 2 <= n < N_U + 2:
                            turn(n - 2)
                        if n >= 3:
                            pv(n - 3)
                        if n == 5:
                            pe.wait_ge(cmp_exp, e_1 + 1)
                            for j in range(2):
                                mm = nc.tensor.transpose(
                                    pb[:, 7, 256 + j * P:256 + (j + 1) * P],
                                    cp[:, 2 * j:2 * j + 2, :, :].rearrange("p a b c -> p (a b c)"), ident)
                            mm.then_inc(cmp_turned, 1)
                        if n == 8:
                            pe.wait_ge(cmp_pt, e_1 + 1)
                            for j in range(2):
                                mm = nc.tensor.matmul(pb[:, 6, j * 256:(j + 1) * 256], cpt[:, j, :],
                                                      vcmp[:, :, :].rearrange("p a b -> p (a b)"), start=True, stop=True)
                            mm.then_inc(cmp_pv, 1)
                        if n == 17:
                            pe.wait_ge(merge_step, (L * 4 + t) * N_MERGE + M_SLC)
                            for i in range(TT):
                                feature_major(4, o_cmp, 0, i, i == 0, False)
                            for i in range(TT):
                                feature_major(4, o_slc, 1, i, False, False)
                        if n == 25:
                            pe.wait_ge(merge_step, (L * 4 + t) * N_MERGE + M_WIN)
                            for i in range(TT):
                                mm = feature_major(4, o_win, 2, i, False, i == TT - 1)
                            mm.then_inc(ot_done, 1)
                    pe.wait_ge(merge_step, (L * 4 + t) * N_MERGE + M_SWA)
                    for i in range(TT):
                        mm = feature_major(5, o_c, 2, i, i == 0, i == TT - 1)
                    mm.then_inc(ot_done, 1)
                    pe.wait_ge(merge_step, (L * 4 + t) * N_MERGE + M_DIFF)
                for t in range(4):
                    pe.wait_ge(sub_step, L * N_SUB + (2 + t))
                    for i in range(TT):
                        mm = nc.tensor.transpose(pb[:, 2 + t, i * P:(i + 1) * P], o_a[:, t, i * P:(i + 1) * P], ident)
                    mm.then_inc(ot_done, 1)

            def merge(L):
                pe.wait_ge(ot_copied, L * 12 + 12)
                pe.sem_inc(passed_pe, 1)
                with pe.Fori(0, KT // 2) as half:
                    m = half * 2
                    for q in range(6):
                        p = P_MIX + q
                        s = 2 * (p % 2)
                        b = 2 * (q % 3)
                        br = (1, 2, 0)[q % 3]
                        split_wait(L, m * 3, p)
                        pe.wait_ge(mix_free, L * 24 + m * 3 + (q + 1))
                        unit_mm(b, s, x_hi, x_lo).then_inc(mix_gate, 1)
                        pe.wait_ge(ob_ready, L * 3 + (q % 3 + 1))
                        unit_mm(b + 1, s + 1, ob_hi[:, 4 * (q % 3):4 * (q % 3) + 4, :],
                                ob_lo[:, 4 * (q % 3):4 * (q % 3) + 4, :], 4).then_inc(pair_done, 1)

            def width_out(L):
                pe.wait_ge(mix_free, L * 24 + (24 + 3))
                pe.wait_ge(z_ready, L * KT + KT)
                for pr in range(PAIRS_WOUT):
                    p = P_WOUT + pr
                    s = 2 * (p % 2)
                    split_wait(L, 0, p)
                    unit_mm(2 * pr, s, z_hi, z_lo).then_inc(y_done, 1)
                    unit_mm(2 * pr + 1, s + 1, z_hi, z_lo).then_inc(pair_done, 1)

            def embed(L):
                pe.wait_ge(p_split, L * 4 + 4)
                for k in range(2):
                    p = P_PLE + k
                    s = 2 * (p % 2)
                    split_wait(L, 0, p)
                    for m in range(KT):
                        if k == 0:
                            pe.wait_ge(resid_ready, L * (3 * KT) + (2 * KT + m + 1))
                        mm = mm3(pb[:, m, :], *blk(s, m), p_hi[:, k, :], p_lo[:, k, :], k == 0, k == 1)
                        if k == 1 and m < KT - 1:
                            mm.then_inc(y_done, 1)
                    mm.then_inc(pair_done, 1)
                for pr in range(PAIRS_PGATE):
                    p = P_PGATE + pr
                    s = 2 * (p % 2)
                    split_wait(L, 0, p)
                    pe.wait_ge(hs_ready, L * KT + KT)
                    pe.wait_ge(pp_ready, L * KT + (2 * pr + 2))
                    unit_mm(2 * pr, s, x_hi, x_lo).then_inc(pgate_even, 1)
                    unit_mm(2 * pr + 1, s + 1, x_hi, x_lo).then_inc(pair_done, 1)

            pe.wait_ge(constants, NCONST)
            with pe.Fori(0, DEPTH) as L:
                ffn(L, 0, P_FFN1, P_OUT1, 0)
                norm(L, 0, resid_ready, 0, 3 * KT)
                projections(L)
                attention(L)
                merge(L)
                width_out(L)
                norm(L, 1, resid_ready, KT, 3 * KT)
                ffn(L, 1, P_FFN2, P_OUT2, 2)
                embed(L)
                norm(L, 2, resid3, 0, KT)

        @block.scalar
        def _(act):
            A = nc.scalar.activation

            def ffn(L, f):
                with act.Fori(0, FT // 2) as half:
                    m = half * 2
                    for q in range(2):
                        act.wait_ge(gate_up_free, L * (2 * FT) + m + (f * FT + q + 1))
                        act.wait_ge(gate_done, L * (2 * FT) + m + (f * FT + q + 1))
                        A(sil[:, q, :], pb[:, 2 * q, :], ACT.Silu).then_inc(silu_done, 1)

            def norm(L, n):
                if n == 0:
                    act.wait_ge(par_loaded, L * 16 + 16)
                    act.wait_ge(xa_done, L * (3 * KT) + KT)
                    A(par_a[:, :], par[:, 0:6 * KT], ACT.Copy, scale=ALPHA).then_inc(par_scaled, 1)
                act.wait_ge(eps_set, 1)
                A(warm[:, :], eps_c[:, 0:1], ACT.Sqrt).then_inc(passed_act, 1)
                for m in range(KT):
                    if m >= 2:
                        act.wait_ge(var_step, L * (3 * KT) + (n * KT + m - 1))
                    act.wait_ge(centered, L * (3 * KT) + (n * KT + m + 1))
                    A(sq[:, m % 2, :], xa[:, m, :], ACT.Square).then_inc(squared, 1)
                act.wait_ge(var_step, L * (3 * KT) + (n * KT + KT))
                A(std[:, :], pb[:, 1, :], ACT.Sqrt, bias=eps_c[:, 0:1]).then_inc(std_done, 1)
                for m in range(KT):
                    g, b = LN_G + n * KT + m, LN_B + n * KT + m
                    if m >= 4:
                        act.wait_ge(x_ready, L * (3 * KT) + (KT + n * KT + m - 3))
                    act.wait_ge(normed, L * (3 * KT) + (n * KT + m + 1))
                    A(tmp[:, m % 4, :], xa[:, m, :], ACT.Identity, bias=par[:, b:b + 1],
                      scale=par[:, g:g + 1]).then_inc(affine, 1)
                    A(x_hi[:, m, :], xa[:, m, :], ACT.Identity, bias=par[:, b:b + 1],
                      scale=par[:, g:g + 1]).then_inc(x_hi_done, 1)
                act.wait_ge(par_scaled, L + 1)
                act.wait_ge(x_hi_done, L * (3 * KT) + (KT + n * KT + KT))
                for m in range(KT):
                    g, b = n * KT + m, LN_B + n * KT + m
                    A(xa[:, m, :], xa[:, m, :], ACT.Identity, bias=par_a[:, b:b + 1],
                      scale=par_a[:, g:g + 1]).then_inc(xa_done, 1)

            def projections(L):
                with act.Fori(0, 3) as half:
                    j = half * 2
                    for q in range(4):
                        if q % 2 == 0:
                            act.wait_ge(proj_even, L * PAIRS_FM + j + (2 + q // 2 + 1))
                        else:
                            act.wait_ge(pair_done, L * PAIRS + j + (P_FM + 2 + q // 2 + 1 + CREDIT))
                        act.sem_inc(passed_act, 1)
                        A(fm[:, j * 2 + q, :], pb[:, q, :], ACT.Copy, scale=SCALE).then_inc(proj_free, 1)
                for q in range(4):
                    if q % 2 == 0:
                        act.wait_ge(proj_even, L * PAIRS_FM + (8 + q // 2 + 1))
                    else:
                        act.wait_ge(pair_done, pairs(L, P_FM + 8 + q // 2))
                    A(fm[:, FM_KA + q, :], pb[:, q, :], ACT.Copy).then_inc(proj_free, 1)
                act.wait_ge(proj_even, L * PAIRS_FM + 11)
                A(fm[:, FM_KS, :], pb[:, 0, :], ACT.Copy).then_inc(proj_free, 1)
                act.wait_ge(pair_done, pairs(L, P_FM + 10))
                A(fm[:, FM_KW, :], pb[:, 1, :], ACT.Copy).then_inc(proj_free, 1)
                act.wait_ge(proj_even, L * PAIRS_FM + 12)
                A(fm[:, FM_KC, :], pb[:, 2, :], ACT.Copy).then_inc(proj_free, 1)
                act.wait_ge(pair_done, pairs(L, P_FM + 11))
                A(gfm, pb[0:24, 3, :], ACT.Sigmoid).then_inc(proj_free, 1)
                A(gfm_slc.rearrange("p (h c) -> p h c", h=16), pb[0:24, 3, :].rearrange("p (c h) -> p h c", h=16),
                  ACT.Sigmoid).then_inc(proj_free, 1)
                for r in range(4):
                    act.wait_ge(hid_done, L * 4 + (r + 1))
                    A(hid_b[:, r:r + 1], pb[:, 4 + r, 62:63], ACT.Copy).then_inc(hid_bias, 1)
                for r in range(4):
                    act.wait_ge(hid_bias, L * 4 + (r + 1))
                    A(hid[:, r, :], pb[:, 4 + r, 0:64], ACT.Gelu_apprx_tanh,
                      bias=hid_b[:, r:r + 1]).then_inc(hid_ready, 1)
                act.wait_ge(cmp_kv_done, L + 1)
                A(kcmp[:, 0:N_CMP], pb[:, 0, 0:N_CMP], ACT.Copy).then_inc(cmp_kv, 1)
                act.wait_ge(vcmp_zeroed, L + 1)
                for r in range(4):
                    h = slice(32 * r, 32 * r + N_CMP)
                    A(vcmp[h, r, :], pb[h, 1, 0:HD], ACT.Copy).then_inc(cmp_kv, 1)
                for br in range(3):
                    src = pb[:, 2, 0:3 * TT * 24].rearrange("p (a i c) -> p a i c", a=3, c=24)[:, br, :, 8 * br:8 * br + 8]
                    A(gate[:, br, :, :, :].rearrange("p a b c -> p a (b c)"), src, ACT.Copy).then_inc(cmp_kv, 1)
                for i in range(TT):
                    if i < TT - 1:
                        act.wait_ge(v_done, L * 3 + (i + 1))
                    else:
                        act.wait_ge(pair_done, pairs(L, P_TM + 3))
                    A(vt[:, i, 0:512], pb[:, 2 * i, :], ACT.Copy).then_inc(v_ready, 1)
                    A(vt[:, i, 512:V_END], pb[:, 2 * i + 1, 0:V_END - 512], ACT.Copy).then_inc(v_ready_b, 1)

            def attention(L):
                act.wait_ge(lam_step, L * 3 + 2)
                A(neglam[:, 0:2], neglam[:, 2:4], ACT.Exp).then_inc(lam_exp, 1)
                with act.Fori(0, 4) as t:
                    e_u = L * (4 * N_U) + t * N_U
                    e_p = L * (4 * N_P) + t * N_P
                    for n, f in enumerate((FM_QB, FM_QC, FM_QA)):
                        A(qst[:, n, :], fm[:, t + f, :], ACT.Copy).then_inc(staged, 1)
                    A(kst[:, :], fm[:, t + FM_KA, :], ACT.Copy).then_inc(staged, 1)
                    for n in range(N_U):
                        kind, i, a = UNITS[n]
                        w = len(key_blocks(kind, i)) * P
                        if n >= 2 and (n - 2) in PIDX:
                            act.wait_ge(pt_done, e_p + (PIDX[n - 2] + 1))
                        elif n >= 2:
                            act.wait_ge(diff_combined, L * 16 + t * 4 + (UNITS[n - 2][1] + 1))
                        act.wait_ge(negmax_done, e_u + (n + 1))
                        A(pE[:, n % 2, 0:w], nS[:, n % 2, 0:w], ACT.Exp, bias=nmx[:, n:n + 1], scale=-1.0,
                          accum_out=lsum[:, n:n + 1]).then_inc(exp_done, 1)
                        if n == 2:
                            act.wait_ge(cmp_step, (L * 4 + t) * N_CS + 3)
                            A(cp[:, :, :, :], cs2[:, :, :, :], ACT.Exp).then_inc(cmp_exp, 1)
                        if n == 7:
                            act.wait_ge(cmp_turned, L * 4 + t + 1)
                            A(cpt[:, :, :].rearrange("p a b -> p (a b)"), pb[:, 7, 256:512], ACT.Copy).then_inc(cmp_pt, 1)
                        if n == 25:
                            act.wait_ge(negmax_done, e_u + 24)
                            for a2 in range(2):
                                A(esk[:, :, a2], nmx[:, 16 + a2:24:2], ACT.Exp, bias=sk[:, a2:a2 + 1]).then_inc(sink_exp, 1)
                    for b in range(2):
                        act.wait_ge(ot_done, L * 12 + t * 2 + (b + 1))
                        act.sem_inc(passed_act, 1)
                        A(fm[:, t + 4 * b, :], pb[:, 4 + b, :], ACT.Copy).then_inc(ot_copied, 1)
                act.wait_ge(merge_step, L * (4 * N_MERGE) + 4 * N_MERGE)
                A(msr[:, :, :], ms[:, :, :], ACT.Sqrt, bias=eps_c[:, 0:1], scale=1.0 / P).then_inc(sub_std, 1)
                for t in range(4):
                    act.wait_ge(ot_done, L * 12 + (8 + t + 1))
                    A(fm[:, FM_QA + t, :], pb[:, 2 + t, :], ACT.Copy, scale=subg[:, 0:1]).then_inc(ot_copied, 1)

            def merge(L):
                with act.Fori(0, KT // 2) as half:
                    m = half * 2
                    for q in range(6):
                        act.wait_ge(mix_free, L * 24 + m * 3 + (q + 1))
                        act.wait_ge(mix_gate, L * 24 + m * 3 + (q + 1))
                        A(sg[:, q % 3, :], pb[:, 2 * (q % 3), :], ACT.Sigmoid).then_inc(sig_done, 1)

            def embed(L):
                act.wait_ge(pair_done, pairs(L, P_OUT2 + 10))
                act.dma_start(p_f[:, :, :], pT[L]).then_inc(p_loaded, 16)
                for m in range(KT):
                    if m < KT - 1:
                        act.wait_ge(y_done, L * Y_LAYER + (7 + 4 + 7 + m + 1))
                    else:
                        act.wait_ge(pair_done, pairs(L, P_PLE + 1))
                    A(pp[:, m, :], pb[:, m, :], ACT.Copy).then_inc(pp_ready, 1)
                for m in range(KT):
                    if m >= 2:
                        act.wait_ge(pg_mul, L * KT + (m - 1))
                    if m % 2 == 0:
                        act.wait_ge(pgate_even, L * 4 + (m // 2 + 1))
                    else:
                        act.wait_ge(pair_done, pairs(L, P_PGATE + m // 2))
                    A(pg[:, m % 2, :], pb[:, m, :], ACT.Sigmoid).then_inc(pg_done, 1)

            act.wait_ge(constants, NCONST)
            with act.Fori(0, DEPTH) as L:
                act.wait_ge(x_ready, L * (3 * KT) + KT)
                act.dma_start(par[:, :], par_d[L]).then_inc(par_loaded, 16)
                ffn(L, 0)
                act.wait_ge(pair_done, pairs(L, P_OUT1 + 10))
                act.dma_start(w1[:, :, :, :], w1_d[L]).then_inc(w1_loaded, 16)
                act.wait_ge(pair_done, pairs(L, P_OUT1 + 10))
                act.dma_start(w2[:, :, :], w2_d[L]).then_inc(w1_loaded, 16)
                norm(L, 0)
                projections(L)
                attention(L)
                merge(L)
                norm(L, 1)
                ffn(L, 1)
                embed(L)
                norm(L, 2)

        @block.vector
        def _(dve):
            V = nc.vector

            def ffn(L, f):
                with dve.Fori(0, FT // 2) as half:
                    m = half * 2
                    for q in range(2):
                        n = f * FT + q
                        dve.wait_ge(pair_done, L * PAIRS + m + ((P_FFN1, P_FFN2)[f] + q + 1 + CREDIT))
                        dve.wait_ge(silu_done, L * (2 * FT) + m + (n + 1))
                        V.tensor_tensor(hf[:, q, :], sil[:, q, :], pb[:, 2 * q + 1, :], ALU.mult).then_inc(gate_up_free, 1)
                        dve.wait_ge(gate_up_free, L * (2 * FT) + m + (n + 1 + 2))
                        V.tensor_scalar(h_hi[:, m + q, :], hf[:, q, :], 1.0, None, ALU.mult).then_inc(h_hi_done, 1)
                        dve.wait_ge(h_hi_done, L * (2 * FT) + m + (n + 1))
                        V.tensor_tensor(h_lo[:, m + q, :], hf[:, q, :], h_hi[:, m + q, :], ALU.subtract).then_inc(h_ready, 1)

            def residual(L, n, factor, wait):
                for m in range(KT):
                    wait(m)
                    V.scalar_tensor_tensor(out=xa[:, m, :], in0=pb[:, m, :], scalar=factor, in1=xa[:, m, :],
                                           op0=ALU.mult, op1=ALU.add).then_inc(resid_ready, 1)

            def norm(L, n):
                dve.wait_ge(mean_done, L * 3 + (n + 1))
                for m in range(KT):
                    V.tensor_tensor(xa[:, m, :], xa[:, m, :], pb[:, 0, :], ALU.subtract).then_inc(centered, 1)
                dve.wait_ge(std_done, L * 3 + (n + 1))
                V.reciprocal(rstd[:, :], std[:, :]).then_inc(rstd_done, 1)
                dve.wait_ge(rstd_done, L * 3 + (n + 1))

                def scale(m):
                    V.tensor_tensor(xa[:, m, :], xa[:, m, :], rstd[:, :], ALU.mult).then_inc(normed, 1)

                scale(0)
                for m in range(KT):
                    if m + 1 < KT:
                        scale(m + 1)
                    dve.wait_ge(x_hi_done, L * (3 * KT) + (KT + n * KT + m + 1))
                    V.tensor_tensor(x_lo[:, m, :], tmp[:, m % 4, :], x_hi[:, m, :], ALU.subtract).then_inc(x_ready, 1)

            def projections(L):
                dve.wait_ge(par_loaded, L * 16 + 16)
                dve.wait_ge(xa_done, L * (3 * KT) + 2 * KT)
                dve.wait_ge(x_ready, L * (3 * KT) + 2 * KT)
                V.tensor_copy(gat[:, :, :, 62:64].rearrange("p a b c -> p (a b) c"),
                              par[:, POS:POS + 64].rearrange("p (a c) -> p a c", c=2)).then_inc(gathered, 1)
                V.memset(vcmp[:, :, :], 0.0).then_inc(vcmp_zeroed, 1)
                for n in range(2):
                    for g in range(2):
                        if g == 0:
                            dve.wait_ge(proj_even, L * PAIRS_FM + (n + 1))
                        else:
                            dve.wait_ge(pair_done, pairs(L, P_FM + n))
                        for r in range(2):
                            h = slice(64 * r, 64 * r + 64)
                            for jj in range(2):
                                src = pb[h, 2 * n + g, :].rearrange("p (c j r) -> p r j c", j=8, r=2)[:, r, :, jj:jj + N_CMP]
                                dst = gat[h, n, 8 * jj:8 * jj + 8, g * N_CMP:(g + 1) * N_CMP]
                                ins = V.tensor_copy(dst, src)
                            ins.then_inc(gathered, 1)

            def attention(L):
                for r in range(2):
                    V.tensor_tensor_reduce(out=lam_t[:, r, :], in0=par[:, LAM + 128 * r:LAM + 128 * r + 64],
                                           in1=par[:, LAM + 128 * r + 64:LAM + 128 * r + 128], scale=1.0, scalar=0.0,
                                           op0=ALU.mult, op1=ALU.add, accum_out=neglam[:, 2 + r:3 + r]).then_inc(lam_step, 1)
                dve.wait_ge(lam_exp, L + 1)
                V.tensor_tensor(neglam[:, 2:3], neglam[:, 1:2], neglam[:, 0:1], ALU.subtract).then_inc(lam_step, 1)
                V.tensor_scalar(subg[:, :], par[:, SUBG:SUBG + 1], par[:, LINIT + 1:LINIT + 2], None,
                                ALU.mult).then_inc(neglam_ready, 1)
                dve.wait_ge(lam_step, L * 3 + 3)
                V.tensor_tensor(neglam[:, 3:4], neglam[:, 2:3], par[:, LINIT:LINIT + 1], ALU.subtract).then_inc(neglam_ready, 1)
                V.memset(kcmp[:, N_CMP:32], 0.0).then_inc(neglam_ready, 1)
                dve.wait_ge(neglam_ready, L * 3 + 3)
                dve.sem_inc(passed_dve, 1)
                with dve.Fori(0, 4) as t:
                    e_u = L * (4 * N_U) + t * N_U
                    e_p = L * (4 * N_P) + t * N_P
                    e_m = (L * 4 + t) * N_MERGE
                    e_c = (L * 4 + t) * N_CS
                    for a in range(2):
                        sl = cst[:, bass.ds(t + (C_SLOPE + 4 * a), 1)]
                        V.tensor_scalar(bias_f[:, a, :], cst[:, C_D:C_D + 512], sl, None, ALU.mult).then_inc(bias_made, 1)
                        V.tensor_scalar(bias_s[:, a, :], cst[:, C_SWA:C_SWA + 256], sl, None, ALU.mult).then_inc(bias_made, 1)
                        V.tensor_scalar(bias_c[:, :, a, :], cst[:, C_CMP:C_CMP + 128].rearrange("p (a b) -> p a b", a=4),
                                        sl, None, ALU.mult).then_inc(bias_made, 1)
                        V.tensor_scalar(sk[:, a:a + 1], par[:, bass.ds(t + (SINK + 4 * a), 1)], 1.0, None,
                                        ALU.mult).then_inc(bias_made, 1)
                        V.tensor_scalar(nsk[:, a:a + 1], par[:, bass.ds(t + (SINK + 4 * a), 1)], -1.0, None,
                                        ALU.mult).then_inc(bias_made, 1)
                    V.tensor_scalar(bias_d[:, :], cst[:, C_D:C_D + 512], cst[:, bass.ds(t + (C_SLOPE + 8), 1)], None,
                                    ALU.mult).then_inc(bias_made, 1)
                    dve.wait_ge(bias_made, (L * 4 + t) * 11 + 11)

                    def negmax(n):
                        kind, i, a = UNITS[n]
                        w = len(key_blocks(kind, i)) * P
                        if kind == SWA:
                            b = bias_s[:, a, 256 - w:256]
                        else:
                            b = (bias_d[:, 0:SEQ] if kind == DIFF else bias_f[:, a, :])[:, SEQ - w:SEQ]
                        if n >= 2:
                            dve.wait_ge(exp_done, e_u + (n - 1))
                        dve.wait_ge(scores_done, e_u + (n + 1))
                        dve.sem_inc(passed_dve, 1)
                        V.tensor_tensor_reduce(out=nS[:, n % 2, 0:w], in0=pb[:, n % 2, 0:w], in1=b, scale=-1.0,
                                               scalar=nsk[:, a:a + 1] if kind == SWA else 3.0e38,
                                               op0=ALU.add, op1=ALU.min,
                                               accum_out=nmx[:, n:n + 1]).then_inc(negmax_done, 1)

                    def combine(n):
                        kind, i, a = UNITS[n]
                        w = (i + 1) * P
                        e_d = (L * 4 + t) * 8 + 2 * i
                        dve.wait_ge(exp_done, e_u + (n + 1))
                        V.reciprocal(rl[:, n:n + 1], lsum[:, n:n + 1]).then_inc(diff_fac, 1)
                        dve.wait_ge(diff_fac, e_d + 1)
                        V.scalar_tensor_tensor(out=dfac[:, i:i + 1], in0=lsum[:, n - 1:n], scalar=neglam[:, 3:4],
                                               in1=rl[:, n:n + 1], op0=ALU.mult, op1=ALU.mult).then_inc(diff_fac, 1)
                        dve.wait_ge(diff_fac, e_d + 2)
                        V.scalar_tensor_tensor(out=pE[:, 1, 0:w], in0=pE[:, 1, 0:w], scalar=dfac[:, i:i + 1],
                                               in1=pE[:, 0, 0:w], op0=ALU.mult, op1=ALU.add).then_inc(diff_combined, 1)

                    def pt_copy(n):
                        if n not in PIDX:
                            return
                        p = PIDX[n]
                        w = len(key_blocks(*UNITS[n][:2])) * P
                        if p >= 2:
                            dve.wait_ge(pv_done, e_p + (p - 1))
                        dve.wait_ge(pt_done, e_p + (p + 1))
                        V.tensor_copy(pt[:, p % 2, 0:w], pb[:, 2 + p % 2, 0:w]).then_inc(pt_copied, 1)

                    step = [0]

                    def merged(ins):
                        step[0] += 1
                        ins.then_inc(merge_step, 1)
                        dve.wait_ge(merge_step, e_m + step[0])

                    def wide(f):
                        return f.unsqueeze(2).to_broadcast([P, 8, HD])

                    def o8(ap):
                        return ap.rearrange("p (a b) -> p a b", b=HD)

                    for n in range(N_U + 3):
                        if n < N_U:
                            negmax(n)
                        if n >= 1 and n - 1 < N_U and UNITS[n - 1][0] == DIFF and UNITS[n - 1][2] == 1:
                            combine(n - 1)
                        if 2 <= n < N_U + 2:
                            pt_copy(n - 2)
                        if n == 0:
                            dve.wait_ge(cmp_scores, L * 4 + t + 1)
                            V.tensor_tensor(cs[:, :, :, :], pb[:, 6:8, 0:P].rearrange("p a (i c) -> p i a c", c=32),
                                            bias_c[:, :, :, :], ALU.add).then_inc(cmp_step, 1)
                            dve.wait_ge(cmp_step, e_c + 1)
                            V.tensor_reduce(cmx[:, :], cs[:, :, :, :].rearrange("p a b c -> p (a b) c"), AX.X,
                                            ALU.max).then_inc(cmp_step, 1)
                            dve.wait_ge(cmp_step, e_c + 2)
                            V.tensor_tensor(cs2[:, :, :, :].rearrange("p a b c -> p (a b) c"),
                                            cs[:, :, :, :].rearrange("p a b c -> p (a b) c"),
                                            cmx[:, :].unsqueeze(2).to_broadcast([P, 8, 32]),
                                            ALU.subtract).then_inc(cmp_step, 1)
                        if n == 6:
                            dve.wait_ge(cmp_exp, L * 4 + t + 1)
                            V.tensor_reduce(csum[:, :], cp[:, :, :, :].rearrange("p a b c -> p (a b) c"), AX.X,
                                            ALU.add).then_inc(cmp_step, 1)
                            dve.wait_ge(cmp_step, e_c + 4)
                            V.reciprocal(crl[:, :], csum[:, :]).then_inc(cmp_step, 1)
                            dve.wait_ge(cmp_step, e_c + 5)
                            V.tensor_tensor(cfac[:, 0, :], crl[:, :], cst[:, C_VALID:C_VALID + 8], ALU.mult).then_inc(cmp_step, 1)
                            dve.wait_ge(cmp_step, e_c + 6)
                            V.tensor_tensor(cfac[:, 1, :].rearrange("p (a b) -> p a b", b=2),
                                            cfac[:, 0, :].rearrange("p (a b) -> p a b", b=2),
                                            gate[:, 0, :, :, t], ALU.mult).then_inc(cmp_step, 1)
                        if n == 12:
                            dve.wait_ge(cmp_pv, L * 4 + t + 1)
                            dve.wait_ge(cmp_step, e_c + 7)
                            merged(V.tensor_tensor(o8(o_cmp[:, :]), o8(pb[:, 6, :]), wide(cfac[:, 1, :]), ALU.mult))
                        if n in (14, 22):
                            br = {14: 1, 22: 2}[n]
                            u0 = 8 * (br - 1)
                            dve.wait_ge(exp_done, e_u + (u0 + 8))
                            merged(V.reciprocal(rl[:, u0:u0 + 8], lsum[:, u0:u0 + 8]))
                            merged(V.tensor_tensor(fac[:, br, :].rearrange("p (a b) -> p a b", b=2),
                                                   rl[:, u0:u0 + 8].rearrange("p (a b) -> p a b", b=2),
                                                   gate[:, br, :, :, t], ALU.mult))
                            dve.wait_ge(pv_done, e_p + (u0 + 8))
                            o = o_slc if br == 1 else o_win
                            merged(V.tensor_tensor(o8(o[:, :]), o8(pb[:, 3 + br, :]), wide(fac[:, br, :]), ALU.mult))
                        if n == 30:
                            dve.wait_ge(sink_exp, L * 8 + t * 2 + 2)
                            merged(V.tensor_tensor(lswa[:, :], lsum[:, 16:24], esk[:, :, :].rearrange("p a b -> p (a b)"), ALU.add))
                            merged(V.reciprocal(rl[:, 16:24], lswa[:, :]))
                            dve.wait_ge(pv_done, e_p + 24)
                            dve.wait_ge(ot_done, L * 12 + t * 2 + 1)
                            merged(V.tensor_tensor(o8(o_c[:, :]), o8(pb[:, 7, :]), wide(rl[:, 16:24]), ALU.mult))
                    merged(V.reciprocal(dfac[:, :], lsum[:, 24:32:2]))
                    dve.wait_ge(pv_done, e_p + N_P)
                    merged(V.tensor_tensor(o_a[:, t, :].rearrange("p (a b) -> p a b", b=P),
                                           pb[:, 6, :].rearrange("p (a b) -> p a b", b=P),
                                           dfac[:, :].unsqueeze(2).to_broadcast([P, TT, P]), ALU.mult))
                    merged(V.tensor_tensor(otmp[:, :], o_a[:, t, :], o_a[:, t, :], ALU.mult))
                    dve.sem_inc(passed_dve, 1)
                    merged(V.tensor_reduce(ms[:, t, :], otmp[:, :].rearrange("p (a b) -> p a b", b=P), AX.X, ALU.add))
                    assert step[0] == N_MERGE, step
                dve.wait_ge(sub_std, L + 1)
                V.reciprocal(msr2[:, :, :].rearrange("p a b -> p (a b)"),
                             msr[:, :, :].rearrange("p a b -> p (a b)")).then_inc(sub_step, 1)
                dve.wait_ge(sub_step, L * N_SUB + 1)
                for t in range(4):
                    o = o_a[:, t, :].rearrange("p (a b) -> p a b", b=P)
                    V.tensor_tensor(o, o, msr2[:, t, :].unsqueeze(2).to_broadcast([P, TT, P]), ALU.mult).then_inc(sub_step, 1)
                dve.wait_ge(ot_copied, L * 12 + 12)
                for n, f in enumerate((FM_QB, FM_QC, FM_QA)):
                    src = fm[:, f:f + 4, :].rearrange("p a b -> p (a b)")
                    hi = ob_hi[:, 4 * n:4 * n + 4, :].rearrange("p a b -> p (a b)")
                    lo = ob_lo[:, 4 * n:4 * n + 4, :].rearrange("p a b -> p (a b)")
                    V.tensor_copy(hi, src).then_inc(ob_hi_done, 1)
                    dve.wait_ge(ob_hi_done, L * 3 + (n + 1))
                    V.tensor_tensor(lo, src, hi, ALU.subtract).then_inc(ob_ready, 1)

            def merge(L):
                dve.wait_ge(ob_ready, L * 3 + 3)
                dve.sem_inc(passed_dve, 1)
                with dve.Fori(0, KT // 2) as half:
                    m = half * 2
                    for q in range(6):
                        zz = zt[:, q // 3, :]
                        dve.wait_ge(pair_done, L * PAIRS + m * 3 + (P_MIX + q + 1 + CREDIT))
                        dve.wait_ge(sig_done, L * 24 + m * 3 + (q + 1))
                        V.tensor_tensor(zz if q % 3 == 0 else gy[:, :], sg[:, q % 3, :], pb[:, 2 * (q % 3) + 1, :],
                                        ALU.mult).then_inc(mix_free, 1)
                        dve.wait_ge(mix_free, L * 24 + m * 3 + (q + 1 + 3))
                        if q % 3:
                            V.tensor_tensor(zz, zz, gy[:, :], ALU.add).then_inc(mix_step, 1)
                            dve.wait_ge(mix_step, L * 16 + m * 2 + (2 * (q // 3) + q % 3))
                        if q % 3 == 2:
                            V.tensor_scalar(z_hi[:, m + q // 3, :], zz, 1.0, None, ALU.mult).then_inc(z_hi_done, 1)
                            dve.wait_ge(z_hi_done, L * KT + m + (q // 3 + 1))
                            V.tensor_tensor(z_lo[:, m + q // 3, :], zz, z_hi[:, m + q // 3, :], ALU.subtract).then_inc(z_ready, 1)

            def embed(L):
                for m in range(KT):
                    dve.wait_ge(resid_ready, L * (3 * KT) + (2 * KT + m + 1))
                    V.tensor_copy(x_hi[:, m, :], xa[:, m, :]).then_inc(hs_hi, 1)
                    dve.wait_ge(hs_hi, L * KT + (m + 1))
                    V.tensor_tensor(x_lo[:, m, :], xa[:, m, :], x_hi[:, m, :], ALU.subtract).then_inc(hs_ready, 1)
                    if m == 3:
                        dve.wait_ge(p_loaded, L * 16 + 16)
                        for k in range(2):
                            V.tensor_copy(p_hi[:, k, :], p_f[:, k, :]).then_inc(p_split, 1)
                            dve.wait_ge(p_split, L * 4 + (2 * k + 1))
                            V.tensor_tensor(p_lo[:, k, :], p_f[:, k, :], p_hi[:, k, :], ALU.subtract).then_inc(p_split, 1)
                for m in range(KT):
                    dve.wait_ge(pg_done, L * KT + (m + 1))
                    V.tensor_tensor(pgp[:, m % 2, :], pg[:, m % 2, :], pp[:, m, :], ALU.mult).then_inc(pg_mul, 1)
                    dve.wait_ge(pg_mul, L * KT + (m + 1))
                    V.tensor_tensor(xa[:, m, :], xa[:, m, :], pgp[:, m % 2, :], ALU.add).then_inc(resid3, 1)

            V.memset(eps_c[:, :], EPS).then_inc(eps_set, 1)
            for n, ring in enumerate((gate_up_free,) * 2 + (proj_free,) * 4 + (mix_free,) * 3):
                V.memset(credit[:, 4 + n:5 + n], 0.0).then_inc(ring, 1)
            dve.wait_ge(constants, NCONST)
            for m in range(KT):
                V.tensor_copy(x_hi[:, m, :], xa[:, m, :]).then_inc(x_hi_done, 1)
                dve.wait_ge(x_hi_done, m + 1)
                V.tensor_tensor(x_lo[:, m, :], xa[:, m, :], x_hi[:, m, :], ALU.subtract).then_inc(x_ready, 1)
            for m in range(KT):
                dve.wait_ge(x_ready, m + 1)
                V.tensor_scalar(xa[:, m, :], xa[:, m, :], ALPHA, None, ALU.mult).then_inc(xa_done, 1)

            with dve.Fori(0, DEPTH) as L:
                def after_ffn(p_last, y0):
                    def wait(m):
                        if m < KT - 1:
                            dve.wait_ge(y_done, L * Y_LAYER + (y0 + m + 1))
                        else:
                            dve.wait_ge(pair_done, pairs(L, p_last))
                    return wait

                def after_width(m):
                    if m % 2 == 0:
                        dve.wait_ge(y_done, L * Y_LAYER + (7 + m // 2 + 1))
                    else:
                        dve.wait_ge(pair_done, pairs(L, P_WOUT + m // 2))

                ffn(L, 0)
                dve.wait_ge(xa_done, L * (3 * KT) + KT)
                residual(L, 0, 0.5, after_ffn(P_OUT1 + 10, 0))
                norm(L, 0)
                projections(L)
                attention(L)
                merge(L)
                dve.wait_ge(xa_done, L * (3 * KT) + 2 * KT)
                residual(L, 1, 1.0, after_width)
                norm(L, 1)
                ffn(L, 1)
                dve.wait_ge(xa_done, L * (3 * KT) + 3 * KT)
                residual(L, 2, 0.5, after_ffn(P_OUT2 + 10, 11))
                embed(L)
                norm(L, 2)
            dve.wait_ge(xa_done, (3 * DEPTH + 1) * KT)
            dve.wait_ge(x_ready, (3 * DEPTH + 1) * KT)
            for m in range(KT):
                V.tensor_tensor(xa[:, m, :], x_hi[:, m, :], x_lo[:, m, :], ALU.add).then_inc(final_done, 1)


def _units(w):
    k, m = w.shape
    return w.reshape(k // P, P, m // P, P).transpose(2, 1, 0, 3).reshape(m // P, P, k)


def _paired(units):
    n, p, c = units.shape
    return units.reshape(n // 2, 2, p, c).transpose(0, 2, 1, 3).reshape(n // 2, p, 2 * c)


def _constants():
    c = np.zeros((P, N_CST), np.float32)
    p = np.arange(P)[:, None]

    def masked(dist, valid):
        return np.where(valid, dist, BIG).astype(np.float32)

    d = p - np.arange(SEQ)[None] + (SEQ - P)
    c[:, C_D:C_D + SEQ] = masked(d, d >= 0)
    d = p - np.arange(256)[None] + P
    c[:, C_SWA:C_SWA + 256] = masked(d, (d >= 0) & (d < 128))
    for i in range(TT):
        blk = np.arange(32)[None]
        d = P * i + p - 16 * blk - 31
        c[:, C_CMP + 32 * i:C_CMP + 32 * (i + 1)] = masked(d, (d >= 0) & (blk < N_CMP))
        c[:, C_VALID + 2 * i:C_VALID + 2 * i + 2] = (P * i + p >= 31)
    c[:, C_ID:C_ID + P] = np.eye(P)
    c[:, C_ONE:C_ONE + P] = 1.0 / D
    c[:, C_SLOPE:C_SLOPE + 8] = [-2.0 ** -(h + 1) for h in range(8)]
    c[:, C_SLOPE + 8:C_SLOPE + 12] = [-2.0 ** (-2 * (h + 1)) for h in range(4)]
    return c


def kernel(**inputs):
    import concourse.bacc as _bacc
    from concourse.bass_utils import run_bass_kernel_spmd as _run

    a = {k: np.asarray(v) for k, v in inputs.items()}
    rows = lambda x: np.ascontiguousarray(x.T.reshape(-1, P, SEQ).transpose(1, 0, 2))
    heads = np.concatenate([np.r_[64 * r:64 * r + 64, 64 * (r + 4):64 * (r + 4) + 64] for r in range(4)])

    par = np.zeros((DEPTH, P, N_PAR), np.float32)
    w1, w2 = [], []
    ffn_in, ffn_out, proj_fm, proj_tm, mix, wout, ple_in, ple_gate = ([] for _ in range(8))
    for L in range(DEPTH):
        for n in range(3):
            par[L, :, LN_G + 8 * n:LN_G + 8 * n + 8] = a["ln_g"][L, n].reshape(KT, P).T
            par[L, :, LN_B + 8 * n:LN_B + 8 * n + 8] = a["ln_b"][L, n].reshape(KT, P).T
        par[L, :, LAM:LAM + 256] = a["diff_lam"][L].reshape(1, 256)
        par[L, :, SINK:SINK + 8] = a["swa_sinks"][L][None]
        par[L, :, SUBG] = a["diff_subln_g"][L]
        li = 0.8 - 0.6 * math.exp(-0.3 * L)
        par[L, :, LINIT], par[L, :, LINIT + 1] = li, 1.0 - li
        pos = a["nsa_cmp_pos"][L].reshape(2, 16, 2, HD).transpose(2, 3, 0, 1).reshape(P, 32)
        par[L, :, POS:POS + 64] = np.repeat(pos, 2, axis=1)
        w1.append(a["nsa_cmp_w1"][L].reshape(2, 16, P, 256).transpose(2, 0, 1, 3))
        w2.append(a["nsa_cmp_w2"][L].reshape(4, P, HD).transpose(1, 0, 2))
        for f in range(2):
            w = a["ffn_w_in"][L, f]
            g, u = _units(w[:, :D_FF]), _units(w[:, D_FF:])
            ffn_in.append(np.concatenate([g, u], axis=2))
            ffn_out.append(_paired(a["ffn_w_out"][L, f].reshape(FT, P, D)))
        w = a["w_in"][L]
        kvc = w[:, B_KVC:B_KVC + 256].reshape(D, 4, HD)
        cols = [np.concatenate([kvc[:, i], kvc[:, i]], axis=1) for i in range(4)]
        cols += [w[:, B_Q:B_Q + 512][:, heads], w[:, C_Q:C_Q + 512][:, heads], w[:, A_Q:A_Q + 512],
                 w[:, A_K:A_K + 512], w[:, B_KVS:B_KVS + 128], w[:, B_KVW:B_KVW + 128],
                 w[:, C_K:C_K + 128], w[:, B_G:B_G + 24], np.zeros((D, P - 24), np.float32)]
        proj_fm.append(_paired(_units(np.concatenate(cols, axis=1))))
        cols = [w[:, A_V:A_V + 512], w[:, B_KVS + 128:B_KVS + 256], w[:, B_KVW + 128:B_KVW + 256],
                w[:, C_V:C_V + 128], np.zeros((D, UNIT - V_END), np.float32)]
        proj_tm.append(_paired(np.concatenate(cols, axis=1).reshape(KT, P, UNIT)))
        gates, branches = [], []
        for br in (1, 2, 0):
            gates.append(_units(w[:, M_G + D * br:M_G + D * (br + 1)]))
            wb = a["w_branch"][L, br]
            branches.append(_units(wb if br == 0 else wb[heads]))
        m = np.concatenate([np.stack(gates, 1), np.stack(branches, 1)], axis=3)
        mix.append(m.reshape(PAIRS_MIX, P, UNIT + UNIT // 2))
        wout.append(_paired(_units(a["w_out"][L])))
        ple_in.append(a["ple_w_in"][L].reshape(2, P, D))
        ple_gate.append(_paired(_units(a["ple_w_gate"][L])))

    stream = lambda x: np.ascontiguousarray(np.concatenate(x))
    arrays = {
        "xT": rows(a["x"][0]), "pT": np.stack([rows(a["p"][L, 0]) for L in range(DEPTH)]),
        "cst": _constants(), "par": par,
        "w1": np.ascontiguousarray(np.stack(w1)), "w2": np.ascontiguousarray(np.stack(w2)),
        "ffn_in": stream(ffn_in), "ffn_out": stream(ffn_out), "proj_fm": stream(proj_fm),
        "proj_tm": stream(proj_tm), "mix": stream(mix), "wout": stream(wout),
        "ple_in": stream(ple_in), "ple_gate": stream(ple_gate),
    }
    nc = _bacc.Bacc("TRN2", target_bir_lowering=False, num_devices=1)
    args = [nc.dram_tensor(f"in_{n}", x.shape, F32, kind="ExternalInput").ap() for n, x in arrays.items()]
    out = nc.dram_tensor("out_0", (P, KT, SEQ), F32, kind="ExternalOutput").ap()
    build(nc, *args, out)
    r = _run(nc, [{f"in_{n}": x for n, x in arrays.items()}], core_ids=[0])
    y = r.results[0]["out_0"]
    return y.transpose(1, 0, 2).reshape(D, SEQ).T.reshape(1, SEQ, D)
```

```python
import math
from contextlib import ExitStack

import numpy as np

import concourse.bass as bass
from concourse import mybir

F32 = mybir.dt.float32
F32R = mybir.dt.float32r
ALU = mybir.AluOpType
ACT = mybir.ActivationFunctionType
AX = mybir.AxisListType

P = 128
D = 1024
SEQ = 512
DEPTH = 2
HD = 64
D_FF = 2816
KT = D // P
FT = D_FF // P
TT = SEQ // P
ALPHA = (2 * DEPTH) ** 0.25
EPS = 1e-5
SCALE = HD ** -0.5
BIG = 1e32
N_CMP = (SEQ - 32) // 16 + 1
UNIT = KT * P

A_Q, A_K, A_V, B_Q, B_KVC, B_KVS, B_KVW, B_G, C_Q, C_K, C_V, M_G = (
    0, 512, 1024, 1536, 2048, 2304, 2560, 2816, 2840, 3352, 3480, 3608)

PAIRS_FFN_IN, PAIRS_FFN_OUT, PAIRS_FM, PAIRS_TM, PAIRS_MIX, PAIRS_WOUT, PAIRS_PLE, PAIRS_PGATE = (
    FT, FT // 2, 12, 4, 24, 4, 2, 4)
P_FFN1 = 0
P_OUT1 = P_FFN1 + PAIRS_FFN_IN
P_FM = P_OUT1 + PAIRS_FFN_OUT
P_TM = P_FM + PAIRS_FM
P_MIX = P_TM + PAIRS_TM
P_WOUT = P_MIX + PAIRS_MIX
P_FFN2 = P_WOUT + PAIRS_WOUT
P_OUT2 = P_FFN2 + PAIRS_FFN_IN
P_PLE = P_OUT2 + PAIRS_FFN_OUT
P_PGATE = P_PLE + PAIRS_PLE
PAIRS = P_PGATE + PAIRS_PGATE
assert PAIRS % 2 == 0
X_PARTS = 4
CREDIT = 2

FM_QB, FM_QC, FM_QA, FM_KA = 0, 4, 8, 12
FM = 16
K_S, K_W, K_C = range(3)
V_A, V_S, V_W, V_C, V_END = 0, 512, 640, 768, 896

LN_G, LN_B, LAM, SINK, SUBG, LINIT, POS = 0, 24, 48, 304, 312, 313, 316
N_PAR = POS + 64
C_D, C_SWA, C_CMP, C_ID, C_ONE, C_SLOPE, C_VALID = 0, 512, 768, 896, 1024, 1152, 1168
N_CST = C_VALID + 8

SLC, WIN, SWA, DIFF = range(4)
UNITS = [(kind, i, a) for kind in (SLC, WIN, SWA, DIFF) for i in range(TT) for a in range(2)]
N_U = len(UNITS)
PU = [n for n, (kind, i, a) in enumerate(UNITS) if kind != DIFF or a == 1]
N_P = len(PU)
PIDX = {n: p for p, n in enumerate(PU)}


N_MERGE, N_CS, N_SUB = 2, 8, 5
LAYER_U = 4 * N_U + 2
N_G = UNITS.index((DIFF, 0, 0))
C_NEG, C_MERGE, C_OT, C_KW = 2, 1, 1, 1
N_FM = FM + 3 + 2
Y_LAYER = 7 + 4 + 7 + 7


def score_bank(n):
    return n - N_U if n >= N_U else (0, 1, 7)[n % 3]


def key_blocks(kind, i):
    return list(range(max(0, i - 1), i + 1)) if kind == SWA else list(range(i + 1))


def build(nc, xT, pT, cst_d, par_d, w1_d, w2_d, ffn_in, ffn_out, proj_fm, proj_tm, mix, wout, ple_in, ple_gate, out):
    ctx = ExitStack()
    with ctx:
        def sb(name, shape, dt=F32, stack=ctx):
            return stack.enter_context(nc.sbuf_tensor(name, shape, dt))

        def sem(name):
            return ctx.enter_context(nc.semaphore(name))

        xa = sb("xa", [P, KT, SEQ])
        x_hi = sb("x_hi", [P, KT, SEQ], F32R)
        x_lo = sb("x_lo", [P, KT, SEQ], F32R)
        with ExitStack() as st:
            slots = [sb(f"q_over_slot_{n}", [P, 2, 2, SEQ], F32R, st) for n in range(2)]
            q_1, q_2 = slots[(P_MIX + 1) % 2], slots[P_MIX % 2]
        raw = sb("raw", [P, 2, 2 * UNIT])
        w_hi = sb("w_hi", [P, 4, UNIT], F32R)
        w_lo = sb("w_lo", [P, 4, UNIT], F32R)
        cst = sb("cst", [P, N_CST])
        par = sb("par", [P, N_PAR])
        with ExitStack() as st:
            p_hi = sb("p_hi", [P, 2, SEQ], F32R, st)
            p_lo = sb("p_lo", [P, 2, SEQ], F32R, st)
        tmp = sb("tmp", [P, 4, SEQ])
        sq = tmp[:, 0:2, :]
        with ExitStack() as st:
            p_f = sb("p_f", [P, 2, SEQ], F32, st)
        std = sb("std", [P, SEQ])
        rstd = sb("rstd", [P, SEQ])
        credit = sb("credit", [P, 20])
        eps_c = sb("eps_c", [P, 1])
        warm = sb("warm", [P, 1])
        par_a = sb("par_a", [P, 6 * KT])

        with ExitStack() as st:
            h_hi = sb("h_hi", [P, FT, SEQ], F32R, st)
            h_lo = sb("h_lo", [P, FT, SEQ], F32R, st)
        sil, hf = sq, tmp[:, 2:4, :]
        with ExitStack() as st:
            pp = sb("pp", [P, KT, SEQ], F32, st)
            pg = sb("pg", [P, 2, SEQ], F32, st)
            pgp = sb("pgp", [P, 2, SEQ], F32, st)
        with ExitStack() as st:
            fm = sb("fm", [P, FM, SEQ], F32, st)
            gate = sb("gate", [P, 3, TT, 2, 4], F32, st)
            hid = sb("hid", [P, 4, 64], F32, st)
            hid_b = sb("hid_b", [P, 4], F32, st)
            w2 = sb("w2", [P, 4, HD], F32, st)
            k_all = sb("k_all", [P, 3, 2, SEQ], F32R, st)
            vcmp = sb("vcmp", [P, 4, HD], F32, st)
            with ExitStack() as s2:
                w1 = sb("w1", [P, 2, 16, 256], F32, s2)
            with ExitStack() as s2:
                vt = sb("vt", [P, TT, V_END], F32, s2)
                k_diff = sb("k_diff", [P, 2, SEQ], F32R, s2)
                kcmp = sb("kcmp", [P, 2, 32], F32R, s2)
                neglam = sb("neglam", [P, 4], F32, s2)
                subg = sb("subg", [P, 1], F32, s2)
                ms = sb("ms", [P, 4, TT], F32, s2)
                msr = sb("msr", [P, 4, TT], F32, s2)
                msr2 = sb("msr2", [P, 4, TT], F32, s2)
                lam_t = sb("lam_t", [P, 2, HD], F32, s2)
                nmx = sb("nmx", [P, N_U], F32, s2)
                lsum = sb("lsum", [P, N_U], F32, s2)
                rl = sb("rl", [P, N_U], F32, s2)
                gate_t = sb("gate_t", [P, 2, TT, 2], F32, s2)
                cmx = sb("cmx", [P, 8], F32, s2)
                csum = sb("csum", [P, 8], F32, s2)
                crl = sb("crl", [P, 8], F32, s2)
                cfac = sb("cfac", [P, 2, 8], F32, s2)
                nsk = sb("nsk", [P, 2], F32, s2)
                dfac = sb("dfac", [P, TT], F32, s2)
                pt = sb("pt", [P, 2, SEQ], F32, s2)
                bias_f = sb("bias_f", [P, 2, SEQ], F32, s2)
                bias_s = sb("bias_s", [P, 2, 256], F32, s2)
                bias_c = sb("bias_c", [P, TT, 2, 32], F32, s2)
                cs = sb("cs", [P, TT, 2, 32], F32, s2)
                cp = sb("cp", [P, TT, 2, 32], F32, s2)
                cpt = sb("cpt", [P, 2, P], F32, s2)
                cs2 = cpt[:, :, :].rearrange("p j (a b c) -> p (j a) b c", a=2, b=2)
                pE2 = sb("pE2", [P, 2, SEQ], F32, s2)
                o_a = sb("o_a", [P, 4, SEQ], F32, s2)
        with ExitStack() as st:
            z_hi = sb("z_hi", [P, KT, SEQ], F32R, st)
            z_lo = sb("z_lo", [P, KT, SEQ], F32R, st)
            ob_hi = sb("ob_hi", [P, 12, SEQ], F32R, st)
            ob_lo = sb("ob_lo", [P, 12, SEQ], F32R, st)
            sg = sb("sg", [P, 3, SEQ], F32, st)
            gy = sb("gy", [P, SEQ], F32, st)
            zt = sb("zt", [P, 2, SEQ], F32, st)
        bias_d, otmp = std, rstd
        gfm, gfm_slc = rstd[0:24, :], std[0:24, :]
        gat = tmp[:, :, :].rearrange("p a b -> p (a b)").rearrange("p (n j c) -> p n j c", n=2, j=16)
        nS = sq

        pb = ctx.enter_context(nc.psum_tensor("pb", [P, 8, SEQ], F32))

        ident = cst[:, C_ID:C_ID + P]
        ones = cst[:, C_ONE:C_ONE + P]

        def pE(n):
            return tmp[:, 2 + n % 4, :] if n % 4 < 2 else pE2[:, n % 4 - 2, :]

        def cols(n):
            kind, i, a = UNITS[n]
            w = len(key_blocks(kind, i)) * P
            return slice(256 - w, 256) if kind == SWA else slice(0, w)

        constants = sem("constants")
        x_loaded = [sem(f"x_loaded_{i}") for i in range(X_PARTS)]
        par_loaded = sem("par_loaded")
        w1_loaded = sem("w1_loaded")
        p_loaded = sem("p_loaded")
        raw_loaded = [sem(f"raw_loaded_{i}") for i in range(2)]
        pair_split = sem("pair_split")
        pair_hi = sem("pair_hi")
        pair_done = sem("pair_done")
        eps_set = sem("eps_set")
        x_hi_done = sem("x_hi_done")
        x_ready = sem("x_ready")
        xa_done = sem("xa_done")
        gate_done = sem("gate_done")
        silu_done = sem("silu_done")
        gate_up_free = sem("gate_up_free")
        h_hi_done = sem("h_hi_done")
        h_ready = sem("h_ready")
        y_done = sem("y_done")
        resid_ready = sem("resid_ready")
        mean_done = sem("mean_done")
        centered = sem("centered")
        squared = sem("squared")
        var_step = sem("var_step")
        std_done = sem("std_done")
        rstd_done = sem("rstd_done")
        normed = sem("normed")
        affine = sem("affine")
        par_scaled = sem("par_scaled")
        proj_even = sem("proj_even")
        proj_free = sem("proj_free")
        gathered = sem("gathered")
        hid_done = sem("hid_done")
        hid_bias = sem("hid_bias")
        hid_ready = sem("hid_ready")
        cmp_kv_done = sem("cmp_kv_done")
        vcmp_zeroed = sem("vcmp_zeroed")
        cmp_kv = sem("cmp_kv")
        v_done = sem("v_done")
        v_ready = sem("v_ready")
        v_ready_b = sem("v_ready_b")
        neglam_ready = sem("neglam_ready")
        lam_step = sem("lam_step")
        lam_exp = sem("lam_exp")
        q_hi = sem("q_hi")
        q_lo = sem("q_lo")
        kw_lo = sem("kw_lo")
        k_split = sem("k_split")
        bias_made = sem("bias_made")
        scores_done = sem("scores_done")
        negmax_done = sem("negmax_done")
        exp_done = sem("exp_done")
        diff_fac = sem("diff_fac")
        diff_combined = sem("diff_combined")
        pt_done = sem("pt_done")
        pt_copied = sem("pt_copied")
        pv_done = sem("pv_done")
        cmp_scores = sem("cmp_scores")
        cmp_step = sem("cmp_step")
        cmp_exp = sem("cmp_exp")
        cmp_turned = sem("cmp_turned")
        cmp_pt = sem("cmp_pt")
        ms_done = sem("ms_done")
        recip_done = sem("recip_done")
        gates_staged = sem("gates_staged")
        scaled = sem("scaled")
        merge_step = sem("merge_step")
        ot_done = sem("ot_done")
        ot_copied = sem("ot_copied")
        sub_step = sem("sub_step")
        sub_std = sem("sub_std")
        ob_hi_done = sem("ob_hi_done")
        ob_ready = sem("ob_ready")
        mix_gate = sem("mix_gate")
        sig_done = sem("sig_done")
        mix_free = sem("mix_free")
        mix_step = sem("mix_step")
        z_hi_done = sem("z_hi_done")
        z_ready = sem("z_ready")
        p_split = sem("p_split")
        pp_ready = sem("pp_ready")
        hs_hi = sem("hs_hi")
        hs_ready = sem("hs_ready")
        pgate_even = sem("pgate_even")
        pg_done = sem("pg_done")
        pg_mul = sem("pg_mul")
        resid3 = sem("resid3")
        final_done = sem("final_done")
        stored = sem("stored")
        passed_pe, passed_act, passed_dve, passed_pool, passed_sp = (
            sem(f"passed_{e}") for e in ("pe", "act", "dve", "pool", "sp"))

        block = ctx.enter_context(nc.Block())

        def in_order(ap, br, i):
            if br == 0:
                return ap[:, i * P:(i + 1) * P]
            if br == 1:
                return ap.rearrange("p (c h) -> p h c", h=16)[:, 4 * i:4 * i + 4, :]
            return ap.rearrange("p (c h) -> p h c", h=4)[:, i, :]

        def pairs(L, p):
            return L * PAIRS + (p + 1 + CREDIT)

        segments = [
            (ffn_in, PAIRS_FFN_IN, lambda L: L * (2 * PAIRS_FFN_IN), 2 * UNIT),
            (ffn_out, PAIRS_FFN_OUT, lambda L: L * (2 * PAIRS_FFN_OUT), 2 * UNIT),
            (proj_fm, PAIRS_FM, lambda L: L * PAIRS_FM, 2 * UNIT),
            (proj_tm, PAIRS_TM, lambda L: L * PAIRS_TM, 2 * UNIT),
            (mix, PAIRS_MIX, lambda L: L * PAIRS_MIX, UNIT + UNIT // 2),
            (wout, PAIRS_WOUT, lambda L: L * PAIRS_WOUT, 2 * UNIT),
            (ffn_in, PAIRS_FFN_IN, lambda L: L * (2 * PAIRS_FFN_IN) + PAIRS_FFN_IN, 2 * UNIT),
            (ffn_out, PAIRS_FFN_OUT, lambda L: L * (2 * PAIRS_FFN_OUT) + PAIRS_FFN_OUT, 2 * UNIT),
            (ple_in, PAIRS_PLE, lambda L: L * PAIRS_PLE, UNIT),
            (ple_gate, PAIRS_PGATE, lambda L: L * PAIRS_PGATE, 2 * UNIT),
        ]

        def own(a):
            return slice(64 * a, 64 * a + 64)

        HALF = SEQ // 2
        STAGES = {
            "k_diff": (k_diff, slice(0, SEQ), FM_KA, 0),
            "q_diff": (q_1, slice(0, SEQ), FM_QA, 0),
            "q_window": (q_2, slice(0, SEQ), FM_QC, 1),
            "q_sparse_0": (q_1, slice(0, HALF), FM_QB, 1),
            "q_sparse_1": (q_1, slice(HALF, SEQ), FM_QB, 1),
        }

        def pieces(name, part):
            dst, cs = STAGES[name][:2]
            if dst is k_diff:
                return [(a, dst[own(a if part == 0 else 1 - a), a, cs], dst[own(a), a, cs]) for a in range(2)]
            return [(a, dst[own(r), a, part, cs], dst[own(a), a, 0, cs]) for a in range(2) for r in range(2)]

        def n_staged(*names):
            return sum(len(pieces(name, 0)) for name in names)

        N_HI, N_LO, N_KW = (n_staged(*STAGES), n_staged("q_diff", "q_sparse_0", "q_sparse_1"),
                            n_staged("k_diff", "q_window"))
        LAYER_HI, LAYER_LO, LAYER_KW = 8 + 4 * N_HI, 8 + 4 * N_LO, 4 * N_KW

        @block.sync
        def _(sp):
            with sp.Fori(0, DEPTH) as L:
                p0 = 0
                for arr, n, first, width in segments:
                    def load(j, p):
                        sp.wait_ge(pair_split, L * PAIRS + j + (p + 1))
                        sp.dma_start(raw[:, p % 2, 0:width], arr[first(L) + j + (p - p0)]).then_inc(raw_loaded[p % 2], 16)

                    if arr is mix:
                        load(0, p0)
                        sp.wait_ge(scores_done, L * LAYER_U + LAYER_U)
                        sp.sem_inc(passed_sp, 1)
                        sp.wait_ge(q_lo, L * LAYER_LO + LAYER_LO)
                        sp.sem_inc(passed_sp, 1)
                        sp.wait_ge(kw_lo, L * LAYER_KW + (LAYER_KW + C_KW))
                        sp.sem_inc(passed_sp, 1)
                        load(0, p0 + 1)
                        with sp.Fori(0, n // 2 - 1) as half:
                            load(half * 2, p0 + 2)
                            load(half * 2, p0 + 3)
                        p0 += n
                        continue
                    with sp.Fori(0, n // 2) as half:
                        j = half * 2
                        load(j, p0)
                        load(j, p0 + 1)
                    if n % 2:
                        load(0, p0 + n - 1)
                    p0 += n
            sp.wait_ge(final_done, KT)
            sp.dma_start(out, xa[:, :, :]).then_inc(stored, 16)
            sp.wait_ge(stored, 16)

        @block.gpsimd
        def _(pool):
            for slot in range(CREDIT):
                nc.gpsimd.memset(credit[:, 2 * slot:2 * slot + 1], 0.0).then_inc(pair_split, 1)
                nc.gpsimd.memset(credit[:, 2 * slot + 1:2 * slot + 2], 0.0).then_inc(pair_done, 1)

            def low(t, hi_count, count, name, ks):
                cs, tile, after = STAGES[name][1:]
                pool.wait_ge(q_hi, hi_count + n_staged(name))
                pool.sem_inc(passed_pool, 1)
                for k in ks:
                    a, dst, hi = pieces(name, 1)[k]
                    nc.gpsimd.tensor_tensor(dst, fm[own(a), t + (tile + after), cs], hi, ALU.subtract).then_inc(kw_lo, 1)
                    pool.wait_ge(kw_lo, count + (k + 1))
                    pool.sem_inc(passed_pool, 1)

            def attention(L):
                with pool.Fori(0, 4) as t:
                    e_hi = L * LAYER_HI + t * N_HI + 8
                    e_kw = L * LAYER_KW + t * N_KW + C_KW
                    pool.wait_ge(gates_staged, (L * 4 + t) * 2 + 2)
                    pool.sem_inc(passed_pool, 1)
                    for n in range(N_G):
                        kind, i, a = UNITS[n]
                        p = pE(n)[:, cols(n)]
                        pool.wait_ge(recip_done, (L * 4 + t) * N_G + (n + 1))
                        pool.sem_inc(passed_pool, 1)
                        g = 1.0 if kind == SWA else gate_t[:, kind, i, a:a + 1]
                        nc.gpsimd.tensor_scalar(p, p, rl[:, n:n + 1], g, ALU.mult, ALU.mult).then_inc(scaled, 1)
                        if n in (7, 10, N_G - 1):
                            pool.wait_ge(scaled, (L * 4 + t) * N_G + (n + 1))
                        if n in (7, 10):
                            low(t, e_hi, e_kw, "k_diff", (n // 10,))
                    low(t, e_hi + n_staged("k_diff", "q_diff"), e_kw + n_staged("k_diff"), "q_window", range(4))

            with pool.Fori(0, DEPTH) as L:
                p0 = 0
                for arr, n, first, width in segments:
                    def split(j, p):
                        s = 2 * (p % 2)
                        src = raw[:, p % 2, 0:width]
                        hi = w_hi[:, s:s + 2, :].rearrange("p a b -> p (a b)")[:, 0:width]
                        lo = w_lo[:, s:s + 2, :].rearrange("p a b -> p (a b)")[:, 0:width]
                        pool.wait_ge(pair_done, L * PAIRS + j + (p + 1))
                        pool.wait_ge(raw_loaded[p % 2], L * (8 * PAIRS) + j * 8 + 16 * (p // 2 + 1))
                        pool.sem_inc(passed_pool, 1)
                        nc.gpsimd.tensor_scalar(hi, src, 1.0, 1.0, ALU.mult, ALU.mult).then_inc(pair_hi, 1)
                        pool.wait_ge(pair_hi, L * PAIRS + j + (p + 1))
                        nc.gpsimd.tensor_tensor(lo, src, hi, ALU.subtract).then_inc(pair_split, 1)

                    if arr is mix:
                        split(0, p0)
                        attention(L)
                        split(0, p0 + 1)
                        with pool.Fori(0, n // 2 - 1) as half:
                            split(half * 2, p0 + 2)
                            split(half * 2, p0 + 3)
                        p0 += n
                        continue
                    with pool.Fori(0, n // 2) as half:
                        j = half * 2
                        split(j, p0)
                        split(j, p0 + 1)
                    if n % 2:
                        split(0, p0 + n - 1)
                    p0 += n

        @block.tensor
        def _(pe):

            def mm3(o, wh, wl, xh, xl, start, stop):
                nc.tensor.matmul(o, wh, xh, start=start, stop=False, skip_group_check=True)
                nc.tensor.matmul(o, wh, xl, start=False, stop=False, skip_group_check=True)
                return nc.tensor.matmul(o, wl, xh, start=False, stop=stop, skip_group_check=True)

            def blk(slot, b):
                return w_hi[:, slot, b * P:(b + 1) * P], w_lo[:, slot, b * P:(b + 1) * P]

            def unit_mm(bank, slot, hi, lo, nk=KT):
                for k in range(nk):
                    last = mm3(pb[:, bank, :], *blk(slot, k), hi[:, k, :], lo[:, k, :], k == 0, k == nk - 1)
                return last

            def as_they_come(ready, base, hi, lo, bank, slot, first_done):
                for k in range(KT):
                    pe.wait_ge(ready, base + (k + 1))
                    for u in range(2):
                        last = mm3(pb[:, bank + u, :], *blk(slot + u, k), hi[:, k, :], lo[:, k, :], k == 0,
                                   k == KT - 1)
                        if k == KT - 1:
                            last.then_inc((first_done, pair_done)[u], 1)

            def split_wait(L, j, p):
                pe.wait_ge(pair_split, L * PAIRS + j + (p + 1 + CREDIT))

            def ffn(L, f, pin, pout, n_x):
                def tile(m, n):
                    b, s = 2 * (n % 2), 2 * ((pin + n) % 2)
                    split_wait(L, m, pin + n)
                    pe.wait_ge(gate_up_free, L * (2 * FT) + m + (f * FT + n + 1))
                    unit_mm(b, s, x_hi, x_lo).then_inc(gate_done, 1)
                    unit_mm(b + 1, s + 1, x_hi, x_lo).then_inc(pair_done, 1)

                split_wait(L, 0, pin)
                pe.wait_ge(gate_up_free, L * (2 * FT) + (f * FT + 1))
                as_they_come(x_ready, L * (3 * KT) + n_x * KT, x_hi, x_lo, 0, 2 * (pin % 2), gate_done)
                tile(0, 1)
                with pe.Fori(0, FT // 2 - 1) as half:
                    tile(half * 2, 2)
                    tile(half * 2, 3)

                def out_pair(j, p, k0, first, last):
                    s = 2 * (p % 2)
                    split_wait(L, j, p)
                    pe.wait_ge(h_ready, L * (2 * FT) + j * 2 + (f * FT + 2 * (k0 + 1)))
                    if first:
                        order = [(u, m) for u in range(2) for m in (4, 5, 6, 7, 0, 1, 2, 3)]
                    elif last:
                        order = [(u, m) for m in range(KT) for u in range(2)]
                    else:
                        order = [(u, m) for u in range(2) for m in range(KT)]
                    for n, (u, m) in enumerate(order):
                        if first and n == 4:
                            pe.wait_ge(gate_up_free, L * (2 * FT) + (f * FT + FT + 2))
                        k = j * 2 + (2 * k0 + u)
                        mm = mm3(pb[:, m, :], *blk(s + u, m), h_hi[:, k, :], h_lo[:, k, :],
                                 first and u == 0, last and u == 1)
                        if last and u == 1 and m < KT - 1:
                            mm.then_inc(y_done, 1)
                    mm.then_inc(pair_done, 1)

                out_pair(0, pout, 0, True, False)
                with pe.Fori(0, 4) as half:
                    j = half * 2
                    out_pair(j, pout + 1, 1, False, False)
                    out_pair(j, pout + 2, 2, False, False)
                out_pair(0, pout + 9, 9, False, False)
                out_pair(0, pout + 10, 10, False, True)

            def norm(L, n, src, base, per_layer):
                for m in range(KT):
                    pe.wait_ge(src, L * per_layer + (base + m + 1))
                    mm = nc.tensor.matmul(pb[:, 0, :], ones, xa[:, m, :], start=m == 0, stop=m == KT - 1)
                mm.then_inc(mean_done, 1)
                for m in range(KT):
                    pe.wait_ge(squared, L * (3 * KT) + (n * KT + m + 1))
                    nc.tensor.matmul(pb[:, 1, :], ones, sq[:, m % 2, :], start=m == 0,
                                     stop=m == KT - 1).then_inc(var_step, 1)

            def projections(L):
                split_wait(L, 0, P_FM)
                as_they_come(x_ready, L * (3 * KT) + KT, x_hi, x_lo, 0, 2 * (P_FM % 2), proj_even)
                s = 2 * ((P_FM + 1) % 2)
                split_wait(L, 0, P_FM + 1)
                unit_mm(2, s, x_hi, x_lo).then_inc(proj_even, 1)
                unit_mm(3, s + 1, x_hi, x_lo).then_inc(pair_done, 1)
                pe.wait_ge(gathered, L * 9 + 9)
                pe.sem_inc(passed_pe, 1)
                with pe.Fori(0, 4) as half:
                    j = half * 2
                    for q in range(2):
                        p = P_FM + 2 + q
                        s = 2 * (p % 2)
                        split_wait(L, j, p)
                        pe.wait_ge(proj_free, L * N_FM + j * 2 + (2 * q + 2))
                        unit_mm(2 * q, s, x_hi, x_lo).then_inc(proj_even, 1)
                        unit_mm(2 * q + 1, s + 1, x_hi, x_lo).then_inc(pair_done, 1)
                p = P_FM + 10
                s = 2 * (p % 2)
                split_wait(L, 0, p)
                pe.wait_ge(proj_free, L * N_FM + 18)
                unit_mm(0, s, x_hi, x_lo).then_inc(proj_even, 1)
                unit_mm(1, s + 1, x_hi, x_lo).then_inc(pair_done, 1)
                p = P_FM + 11
                s = 2 * (p % 2)
                split_wait(L, 0, p)
                pe.wait_ge(proj_free, L * N_FM + 20)
                unit_mm(2, s, x_hi, x_lo).then_inc(proj_even, 1)
                for k in range(KT):
                    mm = mm3(pb[0:24, 3, :], w_hi[:, s + 1, k * P:k * P + 24], w_lo[:, s + 1, k * P:k * P + 24],
                             x_hi[:, k, :], x_lo[:, k, :], k == 0, k == KT - 1)
                mm.then_inc(pair_done, 1)

                pe.wait_ge(w1_loaded, L * 32 + 32)
                for n in range(2):
                    for hm in range(2):
                        for j in range(16):
                            mm = nc.tensor.matmul(pb[:, 4 + 2 * n + hm, 0:64], w1[:, n, j, hm * P:(hm + 1) * P],
                                                  gat[:, n, j, :], start=j == 0, stop=j == 15)
                        mm.then_inc(hid_done, 1)
                pe.wait_ge(hid_ready, L * 4 + 4)
                pe.wait_ge(proj_free, L * N_FM + (N_FM + 4))
                pe.wait_ge(k_split, L * 8 + 6)
                pe.sem_inc(passed_pe, 1)
                for br in range(3):
                    for i in range(TT):
                        mm = nc.tensor.transpose(pb[:, 2, (br * TT + i) * 24:(br * TT + i + 1) * 24],
                                                 in_order(gfm_slc, 0, i) if br == 1 else in_order(gfm, br, i),
                                                 ident[0:24, 0:24])
                for g in range(2):
                    for hm in range(2):
                        nc.tensor.matmul(pb[64 * g:64 * g + 64, 0, 0:N_CMP], w2[:, hm, :],
                                         hid[:, hm, g * N_CMP:(g + 1) * N_CMP], start=hm == 0, stop=hm == 1)
                for r in range(4):
                    for hm in range(2):
                        g = r % 2
                        mm = nc.tensor.matmul(pb[32 * r:32 * r + N_CMP, 1, 0:HD],
                                              hid[:, 2 + hm, g * N_CMP:(g + 1) * N_CMP], w2[:, 2 + hm, :],
                                              start=hm == 0, stop=hm == 1)
                mm.then_inc(cmp_kv_done, 1)
                pe.wait_ge(cmp_kv, L * 9 + 9)
                pe.wait_ge(k_split, L * 8 + 8)

                for pr in range(PAIRS_TM):
                    p = P_TM + pr
                    s = 2 * (p % 2)
                    split_wait(L, 0, p)
                    last = pr == PAIRS_TM - 1
                    ui = [(u, i) for i in range(TT) for u in range(2)] if last else \
                         [(u, i) for u in range(2) for i in range(TT)]
                    for u, i in ui:
                        k = 2 * pr + u
                        xh, xl = x_hi[:, k, i * P:(i + 1) * P], x_lo[:, k, i * P:(i + 1) * P]
                        for b, c0, c1 in ((2 * i, 0, 512), (2 * i + 1, 512, V_END)):
                            mm = mm3(pb[:, b, 0:c1 - c0], xh, xl, w_hi[:, s + u, c0:c1], w_lo[:, s + u, c0:c1],
                                     k == 0, k == KT - 1)
                        if last and u == 1 and i < TT - 1:
                            mm.then_inc(v_done, 1)
                    mm.then_inc(pair_done, 1)

            def attention(L):
                pe.wait_ge(v_ready, L * TT + TT)
                pe.wait_ge(v_ready_b, L * TT + TT)
                pe.wait_ge(neglam_ready, L * 3 + 3)
                pe.sem_inc(passed_pe, 1)

                def scores(e_u, n):
                    kind, i, a = UNITS[n % N_U]
                    q = q_2 if kind == SWA else q_1
                    b = key_blocks(kind, i)
                    ks = slice(b[0] * P, (b[-1] + 1) * P)
                    k = k_diff[:, a, ks] if kind == DIFF else k_all[:, {SLC: K_S, WIN: K_W, SWA: K_C}[kind], a, ks]
                    if a == 0:
                        read = n if n % N_U == 0 else n - 1
                        pe.wait_ge(negmax_done, e_u + (read + C_NEG))
                    for part in range(2):
                        mm = nc.tensor.matmul(pb[:, score_bank(n), 0:len(b) * P], q[:, a, part, i * P:(i + 1) * P], k,
                                              start=part == 0, stop=part == 1)
                    mm.then_inc(scores_done, 1)

                pe.wait_ge(q_lo, L * LAYER_LO + 8)
                scores(L * LAYER_U, 0)
                scores(L * LAYER_U, 1)
                with pe.Fori(0, 4) as t:
                    e_u = L * LAYER_U + t * N_U
                    e_p = L * (4 * N_P) + t * N_P
                    e_1 = L * 4 + t
                    e_lo = L * LAYER_LO + t * N_LO + 8
                    e_kw = L * LAYER_KW + t * N_KW + C_KW

                    def turn(n):
                        if n not in PIDX:
                            return
                        p = PIDX[n]
                        kind, i, a = UNITS[n]
                        if kind == DIFF:
                            pe.wait_ge(diff_combined, L * 16 + t * 4 + (i + 1))
                        else:
                            pe.wait_ge(scaled, (L * 4 + t) * N_G + (n + 1))
                        if p >= 2:
                            pe.wait_ge(pt_copied, e_p + (p - 1))
                        c0 = cols(n).start
                        for j in range(len(key_blocks(kind, i))):
                            mm = nc.tensor.transpose(pb[:, 2 + p % 2, j * P:(j + 1) * P],
                                                     pE(n)[:, c0 + j * P:c0 + (j + 1) * P], ident)
                        mm.then_inc(pt_done, 1)

                    def outputs(kind, i, a, v, probs, start):
                        order = {None: 0, SLC: 1, WIN: 2, SWA: 2}[kind]
                        if kind == SLC:
                            probs = probs.rearrange("p (a b) -> p a b", a=4)
                        return nc.tensor.matmul(in_order(pb[64 * a:64 * a + 64, 5 if kind == SWA else 4, :], order, i),
                                                v, probs, start=start, stop=False, skip_group_check=True)

                    def pv(n):
                        if n not in PIDX:
                            return
                        p = PIDX[n]
                        kind, i, a = UNITS[n]
                        pe.wait_ge(pt_copied, e_p + (p + 1))
                        if n == 0:
                            pe.wait_ge(ot_copied, L * 12 + t * 2 + C_OT)
                        blocks = key_blocks(kind, i)
                        for j, b in enumerate(blocks):
                            pj = pt[:, p % 2, j * P:(j + 1) * P]
                            if kind == DIFF:
                                mm = nc.tensor.matmul(pb[:, 6, i * P:(i + 1) * P], pj, vt[:, b, bass.ts(t, P)],
                                                      start=j == 0, stop=j == len(blocks) - 1)
                            else:
                                c = {SLC: V_S, WIN: V_W, SWA: V_C}[kind] + 64 * a
                                mm = outputs(kind, i, a, vt[:, b, c:c + HD], pj, i == 0 and j == 0 and kind != WIN)
                        mm.then_inc(pv_done, 1)

                    for n in range(2, N_U + 5):
                        if n == 4:
                            pe.wait_ge(q_lo, e_lo)
                        if n == UNITS.index((SWA, 0, 0)):
                            pe.wait_ge(kw_lo, e_kw)
                        if n == N_G:
                            pe.wait_ge(q_lo, e_lo + n_staged("q_diff"))
                            pe.wait_ge(kw_lo, e_kw + n_staged("k_diff"))
                        if n == N_U:
                            pe.wait_ge(q_lo, e_lo + n_staged("q_diff", "q_sparse_0"))
                        if n <= N_U and n % 2 == 0:
                            scores(e_u, n)
                            scores(e_u, n + 1)
                        if n == 4:
                            pe.wait_ge(ot_copied, L * 12 + t * 2 + C_OT)
                            pe.wait_ge(merge_step, (L * 4 + t) * N_MERGE + C_MERGE)
                            for i in range(TT):
                                for a in range(2):
                                    for part in range(2):
                                        mm = nc.tensor.matmul(pb[:, 5 + a, i * 32:(i + 1) * 32],
                                                              q_1[:, a, part, i * P:(i + 1) * P], kcmp[:, a, :],
                                                              start=part == 0, stop=part == 1)
                            mm.then_inc(cmp_scores, 1)
                        if n >= 5:
                            pv(n - 5)
                        if 3 <= n < N_U + 3:
                            turn(n - 3)
                        if n == 10:
                            pe.wait_ge(cmp_step, e_1 * N_CS + N_CS)
                            for j in range(2):
                                mm = nc.tensor.transpose(
                                    pb[:, 6, 256 + j * P:256 + (j + 1) * P],
                                    cp[:, 2 * j:2 * j + 2, :, :].rearrange("p a b c -> p (a b c)"), ident)
                            mm.then_inc(cmp_turned, 1)
                        if n == 13:
                            pe.wait_ge(cmp_pt, e_1 + 1)
                            for i in range(TT):
                                for a in range(2):
                                    mm = outputs(None, i, a, vcmp[:, 2 * (i % 2) + a, :], cpt[:, i // 2, :], False)
                for t in range(4):
                    pe.wait_ge(sub_step, L * N_SUB + (2 + t))
                    for i in range(TT):
                        mm = nc.tensor.transpose(pb[:, 2 + t, i * P:(i + 1) * P], o_a[:, t, i * P:(i + 1) * P], ident)
                    mm.then_inc(ot_done, 1)

            def merge(L):
                pe.wait_ge(ot_copied, L * 12 + (12 + C_OT))
                pe.sem_inc(passed_pe, 1)
                with pe.Fori(0, KT // 2) as half:
                    m = half * 2
                    for q in range(6):
                        p = P_MIX + q
                        s = 2 * (p % 2)
                        b = 2 * (q % 3)
                        br = (1, 2, 0)[q % 3]
                        split_wait(L, m * 3, p)
                        pe.wait_ge(mix_free, L * 24 + m * 3 + (q + 1))
                        unit_mm(b, s, x_hi, x_lo).then_inc(mix_gate, 1)
                        pe.wait_ge(ob_ready, L * 3 + (q % 3 + 1))
                        unit_mm(b + 1, s + 1, ob_hi[:, 4 * (q % 3):4 * (q % 3) + 4, :],
                                ob_lo[:, 4 * (q % 3):4 * (q % 3) + 4, :], 4).then_inc(pair_done, 1)

            def width_out(L):
                pe.wait_ge(mix_free, L * 24 + (24 + 1))
                for pr in range(PAIRS_WOUT):
                    p = P_WOUT + pr
                    s = 2 * (p % 2)
                    split_wait(L, 0, p)
                    if pr == 0:
                        as_they_come(z_ready, L * KT, z_hi, z_lo, 0, s, y_done)
                        continue
                    if pr == 2:
                        pe.wait_ge(mix_free, L * 24 + (24 + 3))
                    unit_mm(2 * pr, s, z_hi, z_lo).then_inc(y_done, 1)
                    unit_mm(2 * pr + 1, s + 1, z_hi, z_lo).then_inc(pair_done, 1)

            def embed(L):
                pe.wait_ge(p_split, L * 4 + 4)
                for k in range(2):
                    p = P_PLE + k
                    s = 2 * (p % 2)
                    split_wait(L, 0, p)
                    for m in range(KT):
                        if k == 0:
                            pe.wait_ge(resid_ready, L * (3 * KT) + (2 * KT + m + 1))
                        mm = mm3(pb[:, m, :], *blk(s, m), p_hi[:, k, :], p_lo[:, k, :], k == 0, k == 1)
                        if k == 1 and m < KT - 1:
                            mm.then_inc(y_done, 1)
                    mm.then_inc(pair_done, 1)
                for pr in range(PAIRS_PGATE):
                    p = P_PGATE + pr
                    s = 2 * (p % 2)
                    split_wait(L, 0, p)
                    pe.wait_ge(hs_ready, L * KT + KT)
                    pe.wait_ge(pp_ready, L * KT + (2 * pr + 2))
                    unit_mm(2 * pr, s, x_hi, x_lo).then_inc(pgate_even, 1)
                    unit_mm(2 * pr + 1, s + 1, x_hi, x_lo).then_inc(pair_done, 1)

            with pe.Fori(0, DEPTH) as L:
                ffn(L, 0, P_FFN1, P_OUT1, 0)
                pe.wait_ge(constants, 16)
                norm(L, 0, resid_ready, 0, 3 * KT)
                projections(L)
                attention(L)
                merge(L)
                width_out(L)
                norm(L, 1, resid_ready, KT, 3 * KT)
                ffn(L, 1, P_FFN2, P_OUT2, 2)
                embed(L)
                norm(L, 2, resid3, 0, KT)

        @block.scalar
        def _(act):
            A = nc.scalar.activation

            def ffn(L, f):
                with act.Fori(0, FT // 2) as half:
                    m = half * 2
                    for q in range(2):
                        act.wait_ge(gate_up_free, L * (2 * FT) + m + (f * FT + q + 1))
                        act.wait_ge(gate_done, L * (2 * FT) + m + (f * FT + q + 1))
                        A(sil[:, q, :], pb[:, 2 * q, :], ACT.Silu).then_inc(silu_done, 1)

            def norm(L, n):
                if n == 0:
                    act.wait_ge(par_loaded, L * 16 + 16)
                    act.wait_ge(xa_done, L * (3 * KT) + KT)
                    A(par_a[:, :], par[:, 0:6 * KT], ACT.Copy, scale=ALPHA).then_inc(par_scaled, 1)
                act.wait_ge(eps_set, 1)
                A(warm[:, :], eps_c[:, 0:1], ACT.Sqrt).then_inc(passed_act, 1)
                for m in range(KT):
                    if m >= 2:
                        act.wait_ge(var_step, L * (3 * KT) + (n * KT + m - 1))
                    act.wait_ge(centered, L * (3 * KT) + (n * KT + m + 1))
                    A(sq[:, m % 2, :], xa[:, m, :], ACT.Square).then_inc(squared, 1)
                act.wait_ge(var_step, L * (3 * KT) + (n * KT + KT))
                A(std[:, :], pb[:, 1, :], ACT.Sqrt, bias=eps_c[:, 0:1]).then_inc(std_done, 1)
                for m in range(KT):
                    g, b = LN_G + n * KT + m, LN_B + n * KT + m
                    if m >= 4:
                        act.wait_ge(x_ready, L * (3 * KT) + (KT + n * KT + m - 3))
                    act.wait_ge(normed, L * (3 * KT) + (n * KT + m + 1))
                    A(tmp[:, m % 4, :], xa[:, m, :], ACT.Identity, bias=par[:, b:b + 1],
                      scale=par[:, g:g + 1]).then_inc(affine, 1)
                    A(x_hi[:, m, :], xa[:, m, :], ACT.Identity, bias=par[:, b:b + 1],
                      scale=par[:, g:g + 1]).then_inc(x_hi_done, 1)
                act.wait_ge(par_scaled, L + 1)
                act.wait_ge(x_hi_done, L * (3 * KT) + (KT + n * KT + KT))
                for m in range(KT):
                    g, b = n * KT + m, LN_B + n * KT + m
                    A(xa[:, m, :], xa[:, m, :], ACT.Identity, bias=par_a[:, b:b + 1],
                      scale=par_a[:, g:g + 1]).then_inc(xa_done, 1)

            def first_step(dst, f):
                for a in range(2):
                    for r in range(2):
                        A(dst[own(r), a, 0, :], fm[own(a), f, :], ACT.Copy).then_inc(q_hi, 1)

            def projections(L):
                with act.Fori(0, 3) as half:
                    j = half * 2
                    for q in range(4):
                        if q % 2 == 0:
                            act.wait_ge(proj_even, L * PAIRS_FM + j + (2 + q // 2 + 1))
                        else:
                            act.wait_ge(pair_done, L * PAIRS + j + (P_FM + 2 + q // 2 + 1 + CREDIT))
                        act.sem_inc(passed_act, 1)
                        A(fm[:, j * 2 + q, :], pb[:, q, :], ACT.Copy, scale=SCALE).then_inc(proj_free, 1)
                for q in range(4):
                    if q % 2 == 0:
                        act.wait_ge(proj_even, L * PAIRS_FM + (8 + q // 2 + 1))
                    else:
                        act.wait_ge(pair_done, pairs(L, P_FM + 8 + q // 2))
                    A(fm[:, FM_KA + q, :], pb[:, q, :], ACT.Copy).then_inc(proj_free, 1)
                for n in range(3):
                    if n == 1:
                        act.wait_ge(pair_done, pairs(L, P_FM + 10))
                    else:
                        act.wait_ge(proj_even, L * PAIRS_FM + 11 + n // 2)
                    A(k_all[own(0), n, 0, :], pb[own(0), n, :], ACT.Copy)
                    A(k_all[own(1), n, 1, :], pb[own(1), n, :], ACT.Copy).then_inc(proj_free, 1)
                act.wait_ge(pair_done, pairs(L, P_FM + 11))
                A(gfm, pb[0:24, 3, :], ACT.Sigmoid).then_inc(proj_free, 1)
                A(gfm_slc.rearrange("p (h c) -> p h c", h=16), pb[0:24, 3, :].rearrange("p (c h) -> p h c", h=16),
                  ACT.Sigmoid).then_inc(proj_free, 1)
                for r in range(4):
                    act.wait_ge(hid_done, L * 4 + (r + 1))
                    A(hid_b[:, r:r + 1], pb[:, 4 + r, 62:63], ACT.Copy).then_inc(hid_bias, 1)
                for r in range(4):
                    act.wait_ge(hid_bias, L * 4 + (r + 1))
                    A(hid[:, r, :], pb[:, 4 + r, 0:64], ACT.Gelu_apprx_tanh,
                      bias=hid_b[:, r:r + 1]).then_inc(hid_ready, 1)
                act.wait_ge(cmp_kv_done, L + 1)
                for a in range(2):
                    A(kcmp[own(a), a, 0:N_CMP], pb[own(a), 0, 0:N_CMP], ACT.Copy).then_inc(cmp_kv, 1)
                act.wait_ge(vcmp_zeroed, L + 1)
                for r in range(4):
                    h = slice(32 * r, 32 * r + N_CMP)
                    A(vcmp[h, r, :], pb[h, 1, 0:HD], ACT.Copy).then_inc(cmp_kv, 1)
                for br in range(3):
                    src = pb[:, 2, 0:3 * TT * 24].rearrange("p (a i c) -> p a i c", a=3, c=24)[:, br, :, 8 * br:8 * br + 8]
                    A(gate[:, br, :, :, :].rearrange("p a b c -> p a (b c)"), src, ACT.Copy).then_inc(cmp_kv, 1)
                act.wait_ge(lam_step, L * 3 + 2)
                A(neglam[:, 0:2], neglam[:, 2:4], ACT.Exp).then_inc(lam_exp, 1)
                act.wait_ge(pair_split, pairs(L, P_TM + 3))
                first_step(q_1, FM_QB)
                for i in range(TT):
                    if i == 2:
                        act.wait_ge(pair_split, pairs(L, P_MIX))
                        first_step(q_2, FM_QC)
                    if i < TT - 1:
                        act.wait_ge(v_done, L * 3 + (i + 1))
                    else:
                        act.wait_ge(pair_done, pairs(L, P_TM + 3))
                    A(vt[:, i, 0:512], pb[:, 2 * i, :], ACT.Copy).then_inc(v_ready, 1)
                    A(vt[:, i, 512:V_END], pb[:, 2 * i + 1, 0:V_END - 512], ACT.Copy).then_inc(v_ready_b, 1)

            def attention(L):
                def exponentials(e_u, n):
                    u = n % N_U
                    act.wait_ge(negmax_done, e_u + (n + 1 + C_NEG))
                    c = slice(cols(u).start, cols(u).stop + (1 if UNITS[u][0] == SWA else 0))
                    A(pE(u)[:, c], nS[:, u % 2, c], ACT.Exp, bias=nmx[:, u:u + 1], scale=-1.0,
                      accum_out=lsum[:, u:u + 1]).then_inc(exp_done, 1)

                exponentials(L * LAYER_U, 0)
                exponentials(L * LAYER_U, 1)
                with act.Fori(0, 4) as t:
                    e_u = L * LAYER_U + t * N_U
                    e_p = L * (4 * N_P) + t * N_P
                    for n in range(2, N_U + 2):
                        if n >= 4 and (n - 4) in PIDX:
                            act.wait_ge(pt_done, e_p + (PIDX[n - 4] + 1))
                        elif n >= 4:
                            act.wait_ge(diff_combined, L * 16 + t * 4 + (UNITS[n - 4][1] + 1))
                        exponentials(e_u, n)
                        for name, first in (("k_diff", 3), ("q_diff", 17), ("q_window", 24), ("q_sparse_0", 28),
                                            ("q_sparse_1", 32)):
                            ps = pieces(name, 0)
                            per = 2 if first >= 28 else 1
                            which, tile, after = STAGES[name][1:]
                            for a, dst, _ in ps[(n - first) * per:(n - first + 1) * per] if n >= first else ():
                                A(dst, fm[own(a), t + (tile + after), which], ACT.Copy).then_inc(q_hi, 1)
                        if n == 6:
                            act.wait_ge(cmp_step, (L * 4 + t) * N_CS + 3)
                            A(cp[:, :, :, :], cs2, ACT.Exp).then_inc(cmp_exp, 1)
                        if n == 11:
                            act.wait_ge(cmp_turned, L * 4 + t + 1)
                            A(cpt[:, :, :].rearrange("p a b -> p (a b)"), pb[:, 6, 256:512], ACT.Copy).then_inc(cmp_pt, 1)
                        if n in (21, 29):
                            b = n // 29
                            act.wait_ge(pv_done, e_p + (16 + 8 * b))
                            act.sem_inc(passed_act, 1)
                            A(fm[:, t + 4 * b, :], pb[:, 4 + b, :], ACT.Copy).then_inc(ot_copied, 1)
                    act.wait_ge(pt_done, e_p + N_P)
                    act.wait_ge(merge_step, (L * 4 + t) * N_MERGE + (N_MERGE + C_MERGE))
                    act.sem_inc(passed_act, 1)
                    for i in range(TT):
                        A(otmp[:, i * P:(i + 1) * P], o_a[:, t, i * P:(i + 1) * P], ACT.Square,
                          accum_out=ms[:, t, i:i + 1]).then_inc(ms_done, 1)
                act.wait_ge(ms_done, L * 16 + 16)
                A(msr[:, :, :], ms[:, :, :], ACT.Sqrt, bias=eps_c[:, 0:1], scale=1.0 / P).then_inc(sub_std, 1)
                act.wait_ge(kw_lo, L * LAYER_KW + (LAYER_KW + C_KW))
                for t in range(4):
                    act.wait_ge(ot_done, L * 4 + (t + 1))
                    A(fm[:, FM_QA + t, :], pb[:, 2 + t, :], ACT.Copy, scale=subg[:, 0:1]).then_inc(ot_copied, 1)

            def merge(L):
                with act.Fori(0, KT // 2) as half:
                    m = half * 2
                    for q in range(6):
                        act.wait_ge(mix_free, L * 24 + m * 3 + (q + 1))
                        act.wait_ge(mix_gate, L * 24 + m * 3 + (q + 1))
                        A(sg[:, q % 3, :], pb[:, 2 * (q % 3), :], ACT.Sigmoid).then_inc(sig_done, 1)

            def embed(L):
                for m in range(KT):
                    if m < KT - 1:
                        act.wait_ge(y_done, L * Y_LAYER + (7 + 4 + 7 + m + 1))
                    else:
                        act.wait_ge(pair_done, pairs(L, P_PLE + 1))
                    A(pp[:, m, :], pb[:, m, :], ACT.Copy).then_inc(pp_ready, 1)
                for m in range(KT):
                    if m >= 2:
                        act.wait_ge(pg_mul, L * KT + (m - 1))
                    if m % 2 == 0:
                        act.wait_ge(pgate_even, L * 4 + (m // 2 + 1))
                    else:
                        act.wait_ge(pair_done, pairs(L, P_PGATE + m // 2))
                    A(pg[:, m % 2, :], pb[:, m, :], ACT.Sigmoid).then_inc(pg_done, 1)

            for c in range(X_PARTS):
                m = slice(c * KT // X_PARTS, (c + 1) * KT // X_PARTS)
                act.dma_start(xa[:, m, :], xT[:, m, :]).then_inc(x_loaded[c], 16)
            act.dma_start(cst[:, :], cst_d).then_inc(constants, 16)
            with act.Fori(0, DEPTH) as L:
                act.wait_ge(x_ready, L * (3 * KT) + KT)
                act.dma_start(par[:, :], par_d[L]).then_inc(par_loaded, 16)
                ffn(L, 0)
                act.wait_ge(pair_done, pairs(L, P_OUT1 + 10))
                act.dma_start(w1[:, :, :, :], w1_d[L]).then_inc(w1_loaded, 16)
                act.wait_ge(pair_done, pairs(L, P_OUT1 + 10))
                act.dma_start(w2[:, :, :], w2_d[L]).then_inc(w1_loaded, 16)
                norm(L, 0)
                projections(L)
                attention(L)
                merge(L)
                norm(L, 1)
                act.wait_ge(normed, L * (3 * KT) + 2 * KT)
                act.dma_start(p_f[:, :, :], pT[L]).then_inc(p_loaded, 16)
                ffn(L, 1)
                embed(L)
                norm(L, 2)

        @block.vector
        def _(dve):
            V = nc.vector

            def ffn(L, f):
                with dve.Fori(0, FT // 2) as half:
                    m = half * 2
                    for q in range(2):
                        n = f * FT + q
                        dve.wait_ge(pair_done, L * PAIRS + m + ((P_FFN1, P_FFN2)[f] + q + 1 + CREDIT))
                        dve.wait_ge(silu_done, L * (2 * FT) + m + (n + 1))
                        V.tensor_tensor(hf[:, q, :], sil[:, q, :], pb[:, 2 * q + 1, :], ALU.mult).then_inc(gate_up_free, 1)
                        dve.wait_ge(gate_up_free, L * (2 * FT) + m + (n + 1 + 2))
                        V.tensor_scalar(h_hi[:, m + q, :], hf[:, q, :], 1.0, None, ALU.mult).then_inc(h_hi_done, 1)
                        dve.wait_ge(h_hi_done, L * (2 * FT) + m + (n + 1))
                        V.tensor_tensor(h_lo[:, m + q, :], hf[:, q, :], h_hi[:, m + q, :], ALU.subtract).then_inc(h_ready, 1)

            def residual(L, n, factor, wait):
                for m in range(KT):
                    wait(m)
                    V.scalar_tensor_tensor(out=xa[:, m, :], in0=pb[:, m, :], scalar=factor, in1=xa[:, m, :],
                                           op0=ALU.mult, op1=ALU.add).then_inc(resid_ready, 1)

            def norm(L, n):
                dve.wait_ge(mean_done, L * 3 + (n + 1))
                for m in range(KT):
                    V.tensor_tensor(xa[:, m, :], xa[:, m, :], pb[:, 0, :], ALU.subtract).then_inc(centered, 1)
                dve.wait_ge(std_done, L * 3 + (n + 1))
                V.reciprocal(rstd[:, :], std[:, :]).then_inc(rstd_done, 1)
                dve.wait_ge(rstd_done, L * 3 + (n + 1))

                def scale(m):
                    V.tensor_tensor(xa[:, m, :], xa[:, m, :], rstd[:, :], ALU.mult).then_inc(normed, 1)

                scale(0)
                for m in range(KT):
                    if m + 1 < KT:
                        scale(m + 1)
                    dve.wait_ge(x_hi_done, L * (3 * KT) + (KT + n * KT + m + 1))
                    V.tensor_tensor(x_lo[:, m, :], tmp[:, m % 4, :], x_hi[:, m, :], ALU.subtract).then_inc(x_ready, 1)

            def projections(L):
                dve.wait_ge(par_loaded, L * 16 + 16)
                dve.wait_ge(xa_done, L * (3 * KT) + 2 * KT)
                dve.wait_ge(x_ready, L * (3 * KT) + 2 * KT)
                V.tensor_copy(gat[:, :, :, 62:64].rearrange("p a b c -> p (a b) c"),
                              par[:, POS:POS + 64].rearrange("p (a c) -> p a c", c=2)).then_inc(gathered, 1)
                V.memset(vcmp[:, :, :], 0.0).then_inc(vcmp_zeroed, 1)
                for n in range(2):
                    for g in range(2):
                        if g == 0:
                            dve.wait_ge(proj_even, L * PAIRS_FM + (n + 1))
                        else:
                            dve.wait_ge(pair_done, pairs(L, P_FM + n))
                        for r in range(2):
                            h = slice(64 * r, 64 * r + 64)
                            for jj in range(2):
                                src = pb[h, 2 * n + g, :].rearrange("p (c j r) -> p r j c", j=8, r=2)[:, r, :, jj:jj + N_CMP]
                                dst = gat[h, n, 8 * jj:8 * jj + 8, g * N_CMP:(g + 1) * N_CMP]
                                ins = V.tensor_copy(dst, src)
                            ins.then_inc(gathered, 1)
                for n in range(3):
                    dve.wait_ge(proj_free, L * N_FM + (4 + FM + n + 1))
                    for a in range(2):
                        V.tensor_tensor(k_all[own(1 - a), n, a, :], pb[own(a), n, :], k_all[own(a), n, a, :],
                                        ALU.subtract).then_inc(k_split, 1)
                for a in range(2):
                    dve.wait_ge(cmp_kv, L * 9 + (a + 1))
                    V.tensor_tensor(kcmp[own(1 - a), a, 0:N_CMP], pb[own(a), 0, 0:N_CMP], kcmp[own(a), a, 0:N_CMP],
                                    ALU.subtract).then_inc(k_split, 1)

            def attention(L):
                for r in range(2):
                    V.tensor_tensor_reduce(out=lam_t[:, r, :], in0=par[:, LAM + 128 * r:LAM + 128 * r + 64],
                                           in1=par[:, LAM + 128 * r + 64:LAM + 128 * r + 128], scale=1.0, scalar=0.0,
                                           op0=ALU.mult, op1=ALU.add, accum_out=neglam[:, 2 + r:3 + r]).then_inc(lam_step, 1)
                dve.wait_ge(lam_exp, L + 1)
                V.tensor_tensor(neglam[:, 2:3], neglam[:, 1:2], neglam[:, 0:1], ALU.subtract).then_inc(lam_step, 1)
                V.tensor_scalar(subg[:, :], par[:, SUBG:SUBG + 1], par[:, LINIT + 1:LINIT + 2], None,
                                ALU.mult).then_inc(neglam_ready, 1)
                dve.wait_ge(lam_step, L * 3 + 3)
                V.tensor_tensor(neglam[:, 3:4], neglam[:, 2:3], par[:, LINIT:LINIT + 1], ALU.subtract).then_inc(neglam_ready, 1)
                V.tensor_scalar(kcmp[:, :, N_CMP], par[:, 0:2], 0.0, None, ALU.mult).then_inc(neglam_ready, 1)

                def column(arr, t, c):
                    return arr[:, c:c + 1] if t is None else arr[:, bass.ds(t + c, 1)]

                def bias_full(t, c):
                    for a in range(2):
                        V.tensor_scalar(bias_f[:, a, :], cst[:, C_D:C_D + 512], column(cst, t, C_SLOPE + 4 * a + c),
                                        None, ALU.mult).then_inc(bias_made, 1)

                def bias_cmp(t, c):
                    for a in range(2):
                        V.tensor_scalar(bias_c[:, :, a, :], cst[:, C_CMP:C_CMP + 128].rearrange("p (a b) -> p a b", a=4),
                                        column(cst, t, C_SLOPE + 4 * a + c), None, ALU.mult).then_inc(bias_made, 1)

                def bias_window(t, c):
                    for a in range(2):
                        V.tensor_scalar(bias_s[:, a, :], cst[:, C_SWA:C_SWA + 256], column(cst, t, C_SLOPE + 4 * a + c),
                                        None, ALU.mult).then_inc(bias_made, 1)
                        V.tensor_scalar(nsk[:, a:a + 1], column(par, t, SINK + 4 * a + c), -1.0, None,
                                        ALU.mult).then_inc(bias_made, 1)

                bias_full(None, 0)
                bias_cmp(None, 0)
                bias_window(None, 0)

                def negmax(e_u, n):
                    u = n % N_U
                    kind, i, a = UNITS[u]
                    w = len(key_blocks(kind, i)) * P
                    if kind == SWA:
                        b = bias_s[:, a, 256 - w:256]
                    else:
                        b = (bias_d[:, 0:SEQ] if kind == DIFF else bias_f[:, a, :])[:, SEQ - w:SEQ]
                    if n >= 2:
                        dve.wait_ge(exp_done, e_u + (n - 1))
                    dve.wait_ge(scores_done, e_u + (n + 1))
                    dve.sem_inc(passed_dve, 1)
                    if kind == SWA:
                        V.tensor_scalar(nS[:, u % 2, 256:257], nsk[:, a:a + 1], 1.0, None, ALU.mult)
                    V.tensor_tensor_reduce(out=nS[:, u % 2, cols(u)], in0=pb[:, score_bank(n), 0:w], in1=b, scale=-1.0,
                                           scalar=nsk[:, a:a + 1] if kind == SWA else 3.0e38,
                                           op0=ALU.add, op1=ALU.min,
                                           accum_out=nmx[:, u:u + 1]).then_inc(negmax_done, 1)

                dve.wait_ge(neglam_ready, L * 3 + 3)
                for k, (name, f) in enumerate((("q_diff", FM_QB), ("q_window", FM_QC))):
                    dve.wait_ge(q_hi, L * LAYER_HI + 4 * (k + 1))
                    for a, dst, hi in pieces(name, 1):
                        V.tensor_tensor(dst, fm[own(a), f, :], hi, ALU.subtract).then_inc(q_lo, 1)
                dve.wait_ge(bias_made, L * 44 + 8)
                negmax(L * LAYER_U, 0)
                negmax(L * LAYER_U, 1)
                with dve.Fori(0, 4) as t:
                    e_u = L * LAYER_U + t * N_U
                    e_p = L * (4 * N_P) + t * N_P
                    e_m = (L * 4 + t) * N_MERGE + C_MERGE
                    e_c = (L * 4 + t) * N_CS
                    e_b = L * 44 + t * 9 + 8
                    for br in range(2):
                        V.tensor_scalar(gate_t[:, br, :, :], gate[:, br + 1, :, :, t], 1.0, None,
                                        ALU.mult).then_inc(gates_staged, 1)

                    def combine(n):
                        kind, i, a = UNITS[n]
                        w = (i + 1) * P
                        e_d = (L * 4 + t) * 8 + 2 * i
                        dve.wait_ge(exp_done, e_u + (n + 1))
                        V.reciprocal(rl[:, n:n + 1], lsum[:, n:n + 1]).then_inc(diff_fac, 1)
                        dve.wait_ge(diff_fac, e_d + 1)
                        V.scalar_tensor_tensor(out=dfac[:, i:i + 1], in0=lsum[:, n - 1:n], scalar=neglam[:, 3:4],
                                               in1=rl[:, n:n + 1], op0=ALU.mult, op1=ALU.mult).then_inc(diff_fac, 1)
                        dve.wait_ge(diff_fac, e_d + 2)
                        V.scalar_tensor_tensor(out=pE(n)[:, 0:w], in0=pE(n)[:, 0:w], scalar=dfac[:, i:i + 1],
                                               in1=pE(n - 1)[:, 0:w], op0=ALU.mult, op1=ALU.add).then_inc(diff_combined, 1)

                    def pt_copy(n):
                        if n not in PIDX:
                            return
                        p = PIDX[n]
                        w = len(key_blocks(*UNITS[n][:2])) * P
                        if p >= 2:
                            dve.wait_ge(pv_done, e_p + (p - 1))
                        dve.wait_ge(pt_done, e_p + (p + 1))
                        V.tensor_copy(pt[:, p % 2, 0:w], pb[:, 2 + p % 2, 0:w]).then_inc(pt_copied, 1)

                    step = [0]

                    def merged(ins):
                        step[0] += 1
                        ins.then_inc(merge_step, 1)
                        dve.wait_ge(merge_step, e_m + step[0])

                    for n in range(2, N_U + 5):
                        if n in (N_G, N_U):
                            dve.wait_ge(bias_made, e_b + (1 if n == N_G else 9))
                            dve.sem_inc(passed_dve, 1)
                        if n < N_U + 2:
                            negmax(e_u, n)
                        for name, before, first in (("q_diff", ("k_diff",), 20),
                                                    ("q_sparse_0", ("k_diff", "q_diff", "q_window"), 30),
                                                    ("q_sparse_1", ("k_diff", "q_diff", "q_window", "q_sparse_0"), 34)):
                            step_n = 2 if name == "q_diff" else 1
                            if n in (first, first + step_n):
                                k = 2 * ((n - first) // step_n)
                                which, tile, after = STAGES[name][1:]
                                dve.wait_ge(q_hi, L * LAYER_HI + t * N_HI + (8 + n_staged(*before) + k + 2))
                                for a, dst, hi in pieces(name, 1)[k:k + 2]:
                                    V.tensor_tensor(dst, fm[own(a), t + (tile + after), which], hi,
                                                    ALU.subtract).then_inc(q_lo, 1)
                        if 2 <= n < N_G + 2:
                            dve.wait_ge(exp_done, e_u + (n - 1))
                            V.reciprocal(rl[:, n - 2:n - 1], lsum[:, n - 2:n - 1]).then_inc(recip_done, 1)
                        elif 2 <= n < N_U + 2 and UNITS[n - 2][2] == 1:
                            combine(n - 2)
                        if 4 <= n < N_U + 4:
                            pt_copy(n - 4)
                        if n == 3:
                            V.tensor_scalar(bias_d[:, :], cst[:, C_D:C_D + 512], column(cst, t, C_SLOPE + 8), None,
                                            ALU.mult).then_inc(bias_made, 1)
                        if n == 18:
                            bias_full(t, 1)
                        if n == 12:
                            bias_cmp(t, 1)
                        if n == 26:
                            bias_window(t, 1)
                        if n == 5:
                            dve.wait_ge(cmp_scores, L * 4 + t + 1)
                            V.tensor_tensor(cs[:, :, :, :], pb[:, 5:7, 0:P].rearrange("p a (i c) -> p i a c", c=32),
                                            bias_c[:, :, :, :], ALU.add).then_inc(cmp_step, 1)
                            dve.wait_ge(cmp_step, e_c + 1)
                            V.tensor_reduce(cmx[:, :], cs[:, :, :, :].rearrange("p a b c -> p (a b) c"), AX.X,
                                            ALU.max).then_inc(cmp_step, 1)
                            dve.wait_ge(cmp_step, e_c + 2)
                            V.tensor_tensor(cs2.rearrange("p a b c -> p (a b) c"),
                                            cs[:, :, :, :].rearrange("p a b c -> p (a b) c"),
                                            cmx[:, :].unsqueeze(2).to_broadcast([P, 8, 32]),
                                            ALU.subtract).then_inc(cmp_step, 1)
                        if n == 8:
                            dve.wait_ge(cmp_exp, L * 4 + t + 1)
                            V.tensor_reduce(csum[:, :], cp[:, :, :, :].rearrange("p a b c -> p (a b) c"), AX.X,
                                            ALU.add).then_inc(cmp_step, 1)
                            dve.wait_ge(cmp_step, e_c + 4)
                            V.reciprocal(crl[:, :], csum[:, :]).then_inc(cmp_step, 1)
                            dve.wait_ge(cmp_step, e_c + 5)
                            V.tensor_tensor(cfac[:, 0, :], crl[:, :], cst[:, C_VALID:C_VALID + 8], ALU.mult).then_inc(cmp_step, 1)
                            dve.wait_ge(cmp_step, e_c + 6)
                            V.tensor_tensor(cfac[:, 1, :].rearrange("p (a b) -> p a b", b=2),
                                            cfac[:, 0, :].rearrange("p (a b) -> p a b", b=2),
                                            gate[:, 0, :, :, t], ALU.mult).then_inc(cmp_step, 1)
                            dve.wait_ge(cmp_step, e_c + 7)
                            c8 = cp[:, :, :, :].rearrange("p a b c -> p (a b) c")
                            V.tensor_tensor(c8, c8, cfac[:, 1, :].unsqueeze(2).to_broadcast([P, 8, 32]),
                                            ALU.mult).then_inc(cmp_step, 1)
                    merged(V.reciprocal(dfac[:, :], lsum[:, 24:32:2]))
                    dve.wait_ge(pv_done, e_p + N_P)
                    merged(V.tensor_tensor(o_a[:, t, :].rearrange("p (a b) -> p a b", b=P),
                                           pb[:, 6, :].rearrange("p (a b) -> p a b", b=P),
                                           dfac[:, :].unsqueeze(2).to_broadcast([P, TT, P]), ALU.mult))
                    assert step[0] == N_MERGE, step
                dve.wait_ge(sub_std, L + 1)
                V.reciprocal(msr2[:, :, :].rearrange("p a b -> p (a b)"),
                             msr[:, :, :].rearrange("p a b -> p (a b)")).then_inc(sub_step, 1)
                dve.wait_ge(sub_step, L * N_SUB + 1)
                for t in range(4):
                    o = o_a[:, t, :].rearrange("p (a b) -> p a b", b=P)
                    V.tensor_tensor(o, o, msr2[:, t, :].unsqueeze(2).to_broadcast([P, TT, P]), ALU.mult).then_inc(sub_step, 1)
                dve.wait_ge(ot_copied, L * 12 + (12 + C_OT))
                for n, f in enumerate((FM_QB, FM_QC, FM_QA)):
                    src = fm[:, f:f + 4, :].rearrange("p a b -> p (a b)")
                    hi = ob_hi[:, 4 * n:4 * n + 4, :].rearrange("p a b -> p (a b)")
                    lo = ob_lo[:, 4 * n:4 * n + 4, :].rearrange("p a b -> p (a b)")
                    V.tensor_copy(hi, src).then_inc(ob_hi_done, 1)
                    dve.wait_ge(ob_hi_done, L * 3 + (n + 1))
                    V.tensor_tensor(lo, src, hi, ALU.subtract).then_inc(ob_ready, 1)

            def merge(L):
                dve.wait_ge(ob_ready, L * 3 + 3)
                dve.sem_inc(passed_dve, 1)
                with dve.Fori(0, KT // 2) as half:
                    m = half * 2
                    for q in range(6):
                        zz = zt[:, q // 3, :]
                        dve.wait_ge(pair_done, L * PAIRS + m * 3 + (P_MIX + q + 1 + CREDIT))
                        dve.wait_ge(sig_done, L * 24 + m * 3 + (q + 1))
                        V.tensor_tensor(zz if q % 3 == 0 else gy[:, :], sg[:, q % 3, :], pb[:, 2 * (q % 3) + 1, :],
                                        ALU.mult).then_inc(mix_free, 1)
                        dve.wait_ge(mix_free, L * 24 + m * 3 + (q + 1 + 3))
                        if q % 3:
                            V.tensor_tensor(zz, zz, gy[:, :], ALU.add).then_inc(mix_step, 1)
                            dve.wait_ge(mix_step, L * 16 + m * 2 + (2 * (q // 3) + q % 3))
                        if q % 3 == 2:
                            V.tensor_scalar(z_hi[:, m + q // 3, :], zz, 1.0, None, ALU.mult).then_inc(z_hi_done, 1)
                            dve.wait_ge(z_hi_done, L * KT + m + (q // 3 + 1))
                            V.tensor_tensor(z_lo[:, m + q // 3, :], zz, z_hi[:, m + q // 3, :], ALU.subtract).then_inc(z_ready, 1)

            def embed(L):
                for m in range(KT):
                    dve.wait_ge(resid_ready, L * (3 * KT) + (2 * KT + m + 1))
                    V.tensor_copy(x_hi[:, m, :], xa[:, m, :]).then_inc(hs_hi, 1)
                    dve.wait_ge(hs_hi, L * KT + (m + 1))
                    V.tensor_tensor(x_lo[:, m, :], xa[:, m, :], x_hi[:, m, :], ALU.subtract).then_inc(hs_ready, 1)
                for m in range(KT):
                    dve.wait_ge(pg_done, L * KT + (m + 1))
                    V.tensor_tensor(pgp[:, m % 2, :], pg[:, m % 2, :], pp[:, m, :], ALU.mult).then_inc(pg_mul, 1)
                    dve.wait_ge(pg_mul, L * KT + (m + 1))
                    V.tensor_tensor(xa[:, m, :], xa[:, m, :], pgp[:, m % 2, :], ALU.add).then_inc(resid3, 1)

            V.memset(eps_c[:, :], EPS).then_inc(eps_set, 1)
            for n, ring in enumerate((gate_up_free,) * 2 + (proj_free,) * 4 + (mix_free,) * 3 + (negmax_done,) * C_NEG
                                       + (merge_step,) * C_MERGE + (ot_copied,) * C_OT + (kw_lo,) * C_KW):
                V.memset(credit[:, 4 + n:5 + n], 0.0).then_inc(ring, 1)
            for m in range(KT):
                dve.wait_ge(x_loaded[m * X_PARTS // KT], 16)
                V.tensor_copy(x_hi[:, m, :], xa[:, m, :]).then_inc(x_hi_done, 1)
                dve.wait_ge(x_hi_done, m + 1)
                V.tensor_tensor(x_lo[:, m, :], xa[:, m, :], x_hi[:, m, :], ALU.subtract).then_inc(x_ready, 1)
            for m in range(KT):
                dve.wait_ge(x_ready, m + 1)
                V.tensor_scalar(xa[:, m, :], xa[:, m, :], ALPHA, None, ALU.mult).then_inc(xa_done, 1)

            dve.wait_ge(constants, 16)
            with dve.Fori(0, DEPTH) as L:
                def after_ffn(p_last, y0):
                    def wait(m):
                        if m < KT - 1:
                            dve.wait_ge(y_done, L * Y_LAYER + (y0 + m + 1))
                        else:
                            dve.wait_ge(pair_done, pairs(L, p_last))
                    return wait

                def after_width(m):
                    if m % 2 == 0:
                        dve.wait_ge(y_done, L * Y_LAYER + (7 + m // 2 + 1))
                    else:
                        dve.wait_ge(pair_done, pairs(L, P_WOUT + m // 2))

                ffn(L, 0)
                dve.wait_ge(xa_done, L * (3 * KT) + KT)
                residual(L, 0, 0.5, after_ffn(P_OUT1 + 10, 0))
                norm(L, 0)
                projections(L)
                attention(L)
                merge(L)
                dve.wait_ge(xa_done, L * (3 * KT) + 2 * KT)
                residual(L, 1, 1.0, after_width)
                norm(L, 1)
                ffn(L, 1)
                dve.wait_ge(h_ready, L * (2 * FT) + 2 * FT)
                dve.wait_ge(p_loaded, L * 16 + 16)
                for k in range(2):
                    V.tensor_copy(p_hi[:, k, :], p_f[:, k, :]).then_inc(p_split, 1)
                    dve.wait_ge(p_split, L * 4 + (2 * k + 1))
                    V.tensor_tensor(p_lo[:, k, :], p_f[:, k, :], p_hi[:, k, :], ALU.subtract).then_inc(p_split, 1)
                dve.wait_ge(xa_done, L * (3 * KT) + 3 * KT)
                residual(L, 2, 0.5, after_ffn(P_OUT2 + 10, 11))
                embed(L)
                norm(L, 2)
            dve.wait_ge(xa_done, (3 * DEPTH + 1) * KT)
            dve.wait_ge(x_ready, (3 * DEPTH + 1) * KT)
            for m in range(KT):
                V.tensor_tensor(xa[:, m, :], x_hi[:, m, :], x_lo[:, m, :], ALU.add).then_inc(final_done, 1)


def _units(w):
    k, m = w.shape
    return w.reshape(k // P, P, m // P, P).transpose(2, 1, 0, 3).reshape(m // P, P, k)


def _paired(units):
    n, p, c = units.shape
    return units.reshape(n // 2, 2, p, c).transpose(0, 2, 1, 3).reshape(n // 2, p, 2 * c)


def _constants():
    c = np.zeros((P, N_CST), np.float32)
    p = np.arange(P)[:, None]

    def masked(dist, valid):
        return np.where(valid, dist, BIG).astype(np.float32)

    d = p - np.arange(SEQ)[None] + (SEQ - P)
    c[:, C_D:C_D + SEQ] = masked(d, d >= 0)
    d = p - np.arange(256)[None] + P
    c[:, C_SWA:C_SWA + 256] = masked(d, (d >= 0) & (d < 128))
    for i in range(TT):
        blk = np.arange(32)[None]
        d = P * i + p - 16 * blk - 31
        c[:, C_CMP + 32 * i:C_CMP + 32 * (i + 1)] = masked(d, (d >= 0) & (blk < N_CMP))
        c[:, C_VALID + 2 * i:C_VALID + 2 * i + 2] = (P * i + p >= 31)
    c[:, C_ID:C_ID + P] = np.eye(P)
    c[:, C_ONE:C_ONE + P] = 1.0 / D
    c[:, C_SLOPE:C_SLOPE + 8] = [-2.0 ** -(h + 1) for h in range(8)]
    c[:, C_SLOPE + 8:C_SLOPE + 12] = [-2.0 ** (-2 * (h + 1)) for h in range(4)]
    return c


def kernel(**inputs):
    import concourse.bacc as _bacc
    from concourse.bass_utils import run_bass_kernel_spmd as _run

    a = {k: np.asarray(v) for k, v in inputs.items()}
    rows = lambda x: np.ascontiguousarray(x.T.reshape(-1, P, SEQ).transpose(1, 0, 2))
    heads = np.concatenate([np.r_[64 * r:64 * r + 64, 64 * (r + 4):64 * (r + 4) + 64] for r in range(4)])

    par = np.zeros((DEPTH, P, N_PAR), np.float32)
    w1, w2 = [], []
    ffn_in, ffn_out, proj_fm, proj_tm, mix, wout, ple_in, ple_gate = ([] for _ in range(8))
    for L in range(DEPTH):
        for n in range(3):
            par[L, :, LN_G + 8 * n:LN_G + 8 * n + 8] = a["ln_g"][L, n].reshape(KT, P).T
            par[L, :, LN_B + 8 * n:LN_B + 8 * n + 8] = a["ln_b"][L, n].reshape(KT, P).T
        par[L, :, LAM:LAM + 256] = a["diff_lam"][L].reshape(1, 256)
        par[L, :, SINK:SINK + 8] = a["swa_sinks"][L][None]
        par[L, :, SUBG] = a["diff_subln_g"][L]
        li = 0.8 - 0.6 * math.exp(-0.3 * L)
        par[L, :, LINIT], par[L, :, LINIT + 1] = li, 1.0 - li
        pos = a["nsa_cmp_pos"][L].reshape(2, 16, 2, HD).transpose(2, 3, 0, 1).reshape(P, 32)
        par[L, :, POS:POS + 64] = np.repeat(pos, 2, axis=1)
        w1.append(a["nsa_cmp_w1"][L].reshape(2, 16, P, 256).transpose(2, 0, 1, 3))
        w2.append(a["nsa_cmp_w2"][L].reshape(4, P, HD).transpose(1, 0, 2))
        for f in range(2):
            w = a["ffn_w_in"][L, f]
            g, u = _units(w[:, :D_FF]), _units(w[:, D_FF:])
            ffn_in.append(np.concatenate([g, u], axis=2))
            ffn_out.append(_paired(a["ffn_w_out"][L, f].reshape(FT, P, D)))
        w = a["w_in"][L]
        kvc = w[:, B_KVC:B_KVC + 256].reshape(D, 4, HD)
        cols = [np.concatenate([kvc[:, i], kvc[:, i]], axis=1) for i in range(4)]
        cols += [w[:, B_Q:B_Q + 512][:, heads], w[:, C_Q:C_Q + 512][:, heads], w[:, A_Q:A_Q + 512],
                 w[:, A_K:A_K + 512], w[:, B_KVS:B_KVS + 128], w[:, B_KVW:B_KVW + 128],
                 w[:, C_K:C_K + 128], w[:, B_G:B_G + 24], np.zeros((D, P - 24), np.float32)]
        proj_fm.append(_paired(_units(np.concatenate(cols, axis=1))))
        cols = [w[:, A_V:A_V + 512], w[:, B_KVS + 128:B_KVS + 256], w[:, B_KVW + 128:B_KVW + 256],
                w[:, C_V:C_V + 128], np.zeros((D, UNIT - V_END), np.float32)]
        proj_tm.append(_paired(np.concatenate(cols, axis=1).reshape(KT, P, UNIT)))
        gates, branches = [], []
        for br in (1, 2, 0):
            gates.append(_units(w[:, M_G + D * br:M_G + D * (br + 1)]))
            wb = a["w_branch"][L, br]
            branches.append(_units(wb if br == 0 else wb[heads]))
        m = np.concatenate([np.stack(gates, 1), np.stack(branches, 1)], axis=3)
        mix.append(m.reshape(PAIRS_MIX, P, UNIT + UNIT // 2))
        wout.append(_paired(_units(a["w_out"][L])))
        ple_in.append(a["ple_w_in"][L].reshape(2, P, D))
        ple_gate.append(_paired(_units(a["ple_w_gate"][L])))

    stream = lambda x: np.ascontiguousarray(np.concatenate(x))
    arrays = {
        "xT": rows(a["x"][0]), "pT": np.stack([rows(a["p"][L, 0]) for L in range(DEPTH)]),
        "cst": _constants(), "par": par,
        "w1": np.ascontiguousarray(np.stack(w1)), "w2": np.ascontiguousarray(np.stack(w2)),
        "ffn_in": stream(ffn_in), "ffn_out": stream(ffn_out), "proj_fm": stream(proj_fm),
        "proj_tm": stream(proj_tm), "mix": stream(mix), "wout": stream(wout),
        "ple_in": stream(ple_in), "ple_gate": stream(ple_gate),
    }
    nc = _bacc.Bacc("TRN2", target_bir_lowering=False, num_devices=1)
    args = [nc.dram_tensor(f"in_{n}", x.shape, F32, kind="ExternalInput").ap() for n, x in arrays.items()]
    out = nc.dram_tensor("out_0", (P, KT, SEQ), F32, kind="ExternalOutput").ap()
    build(nc, *args, out)
    r = _run(nc, [{f"in_{n}": x for n, x in arrays.items()}], core_ids=[0])
    y = r.results[0]["out_0"]
    return y.transpose(1, 0, 2).reshape(D, SEQ).T.reshape(1, SEQ, D)
```
